# Optimizing a Trainium2 kernel written in Bass

```python
import functools
import jax, jax.numpy as jnp
from jax import lax
import numpy as np

D_MODEL = 1024
BATCH = 1
SEQ = 256
DEPTH = 1

CHUNK = 64
N_META = 16
META_PAD = CHUNK - N_META
DN_HEADS = 4
DN_DK = 128
DN_DV = 128
DN_QK = DN_HEADS * DN_DK
DN_VW = DN_HEADS * DN_DV
SHORT_CONV = 4
CONV_CH = 512
CONV_WIDTH = 31
IN_SIZES = (DN_QK, DN_QK, DN_VW, DN_HEADS, DN_HEADS, DN_VW, 2 * CONV_CH)
IN_COLS = int(sum(IN_SIZES))
IN_SPLITS = [int(i) for i in np.cumsum(IN_SIZES)[:-1]]
N_EXPERTS = 32
TOP_K = 4
D_FF = 1024
SWIGLU_LIMIT = 7.0
SWIGLU_ALPHA = 1.702
MOE_BLOCK = 256
EPS = 1e-6

kernel_name = "hybrid_deltanet_conformer_moe_block"

def rms_norm(x, g):
    xf = x.astype(jnp.float32)
    y = xf * lax.rsqrt(jnp.mean(xf * xf, axis=-1, keepdims=True) + EPS)
    return (y * g.astype(jnp.float32)).astype(x.dtype)

def layer_norm(x, g, b):
    xf = x.astype(jnp.float32)
    mu = jnp.mean(xf, axis=-1, keepdims=True)
    xc = xf - mu
    y = xc * lax.rsqrt(jnp.mean(xc * xc, axis=-1, keepdims=True) + 1e-5)
    return (y * g.astype(jnp.float32) + b.astype(jnp.float32)).astype(x.dtype)

def l2_norm(x):
    xf = x.astype(jnp.float32)
    return xf * lax.rsqrt(jnp.sum(xf * xf, axis=-1, keepdims=True) + EPS)

def causal_depthwise_conv(x, w):
    k, c = w.shape
    return lax.conv_general_dilated(
        x, w[:, None, :].astype(x.dtype), window_strides=(1,), padding=[(k - 1, 0)],
        dimension_numbers=('NWC', 'WIO', 'NWC'), feature_group_count=c)

def chunked_gated_delta_rule(q, k, v, g, beta):
    b, lp, h, dk = q.shape
    dv = v.shape[-1]
    n = lp // CHUNK

    def blocks(t):
        return jnp.moveaxis(t.reshape((b, n, CHUNK, h) + t.shape[3:]), 3, 2)

    q, k, v, g, beta = (blocks(t) for t in (q, k, v, g, beta))
    g_cum = jnp.cumsum(g, axis=-1)
    incl = jnp.tril(jnp.ones((CHUNK, CHUNK), dtype=bool))
    strict = jnp.tril(jnp.ones((CHUNK, CHUNK), dtype=bool), -1)
    diff = g_cum[..., :, None] - g_cum[..., None, :]
    gamma = jnp.where(incl, jnp.exp(jnp.where(incl, diff, 0.0)), 0.0)
    k_beta = k * beta[..., None]
    a_mat = jnp.where(strict, jnp.einsum('bnhik,bnhjk->bnhij', k_beta, k) * gamma, 0.0)
    t_mat = a_mat + jnp.eye(CHUNK, dtype=a_mat.dtype)
    solve = functools.partial(jax.lax.linalg.triangular_solve, left_side=True, lower=True,
                              unit_diagonal=True)
    u = solve(t_mat, v * beta[..., None])
    w = solve(t_mat, k_beta * jnp.exp(g_cum)[..., None])
    qk = jnp.einsum('bnhik,bnhjk->bnhij', q, k) * gamma
    q_dec = q * jnp.exp(g_cum)[..., None]
    k_dec = k * jnp.exp(g_cum[..., -1:] - g_cum)[..., None]
    chunk_decay = jnp.exp(g_cum[..., -1])

    def step(state, inp):
        u_c, w_c, qk_c, qd_c, kd_c, dec_c = inp
        v_new = u_c - jnp.einsum('bhck,bhkv->bhcv', w_c, state)
        o_c = (jnp.einsum('bhck,bhkv->bhcv', qd_c, state)
               + jnp.einsum('bhij,bhjv->bhiv', qk_c, v_new))
        state = state * dec_c[..., None, None] + jnp.einsum('bhck,bhcv->bhkv', kd_c, v_new)
        return state, o_c

    xs = tuple(jnp.moveaxis(t, 1, 0) for t in (u, w, qk, q_dec, k_dec, chunk_decay))
    s0 = jnp.zeros((b, h, dk, dv), jnp.float32)
    _, o = lax.scan(step, s0, xs)
    o = jnp.moveaxis(o, 0, 1)
    return jnp.moveaxis(o, 2, 3).reshape(b, lp, h, dv)

def mixer_block(hn, w_in, conv_qkv_w, a_log, dt_bias, dn_norm_g, w_dn_out, b_glu,
                conv_dw_w, conv_dw_b, conv_ln_g, conv_ln_b, w_conv_out, b_conv_out,
                w_merge, b_merge, w_out):
    bsz, length, _ = hn.shape
    dt = hn.dtype
    proj = hn @ w_in
    q_p, k_p, v_p, a_p, b_p, go_p, glu_p = jnp.split(proj, IN_SPLITS, axis=-1)

    qkv = jnp.concatenate([q_p, k_p, v_p], axis=-1)
    qkv = jnp.pad(qkv, ((0, 0), (META_PAD, 0), (0, 0)))
    qkv = jax.nn.silu(causal_depthwise_conv(qkv, conv_qkv_w))
    lp = length + META_PAD
    q, k, v = jnp.split(qkv, [DN_QK, 2 * DN_QK], axis=-1)
    q = l2_norm(q.reshape(bsz, lp, DN_HEADS, DN_DK)) * (DN_DK ** -0.5)
    k = l2_norm(k.reshape(bsz, lp, DN_HEADS, DN_DK))
    v = v.reshape(bsz, lp, DN_HEADS, DN_DV).astype(jnp.float32)
    beta = jax.nn.sigmoid(b_p.astype(jnp.float32))
    g = -jnp.exp(a_log.astype(jnp.float32)) * jax.nn.softplus(
        a_p.astype(jnp.float32) + dt_bias.astype(jnp.float32))
    pad3 = ((0, 0), (META_PAD, 0), (0, 0))
    beta = jnp.pad(beta, pad3)
    g = jnp.pad(g, pad3)
    o = chunked_gated_delta_rule(q, k, v, g, beta)[:, META_PAD:]
    o = rms_norm(o, dn_norm_g).astype(dt)
    o = o * jax.nn.silu(go_p.reshape(bsz, length, DN_HEADS, DN_DV))
    y_a = o.reshape(bsz, length, DN_VW) @ w_dn_out

    u = glu_p + b_glu
    u = u[..., :CONV_CH] * jax.nn.sigmoid(u[..., CONV_CH:])
    u = causal_depthwise_conv(u, conv_dw_w) + conv_dw_b
    u = jax.nn.silu(layer_norm(u, conv_ln_g, conv_ln_b))
    y_b = u @ w_conv_out + b_conv_out

    gates = jax.nn.sigmoid(hn @ w_merge + b_merge)
    y = gates[..., :D_MODEL] * y_a + gates[..., D_MODEL:] * y_b
    return y @ w_out

def moe_ffn(hn, w_router, b_router, w_gate_up, b_gate_up, w_down, b_down):
    bsz, length, d = hn.shape
    tokens = hn.reshape(-1, d)
    t = tokens.shape[0]
    logits = tokens @ w_router + b_router
    top_vals, top_idx = lax.top_k(logits, TOP_K)
    gates = jax.nn.softmax(top_vals.astype(jnp.float32), axis=-1).astype(hn.dtype)
    m = t * TOP_K
    flat_e = top_idx.reshape(-1).astype(jnp.int32)
    flat_tok = jnp.repeat(jnp.arange(t, dtype=jnp.int32), TOP_K)
    order = jnp.argsort(flat_e, stable=True)
    sorted_e = flat_e[order]
    counts = jnp.bincount(flat_e, length=N_EXPERTS)
    padded = (counts + MOE_BLOCK - 1) // MOE_BLOCK * MOE_BLOCK
    starts = jnp.cumsum(counts) - counts
    pstarts = jnp.cumsum(padded) - padded
    dest = pstarts[sorted_e] + (jnp.arange(m, dtype=jnp.int32) - starts[sorted_e])
    n_blocks = -(-m // MOE_BLOCK) + N_EXPERTS
    cap = n_blocks * MOE_BLOCK
    tok_buf = jnp.full((cap,), t, jnp.int32).at[dest].set(flat_tok[order])
    gate_buf = jnp.zeros((cap,), hn.dtype).at[dest].set(gates.reshape(-1)[order])
    block_e = jnp.minimum(
        jnp.searchsorted(jnp.cumsum(padded), jnp.arange(n_blocks, dtype=jnp.int32) * MOE_BLOCK,
                         side='right'), N_EXPERTS - 1)
    tokens_pad = jnp.concatenate([tokens, jnp.zeros((1, d), hn.dtype)], axis=0)
    x_blocks = tokens_pad[tok_buf].reshape(n_blocks, MOE_BLOCK, d)

    def expert_block(args):
        xb, e = args
        gu = xb @ w_gate_up[e] + b_gate_up[e]
        gate = jnp.minimum(gu[:, :D_FF], SWIGLU_LIMIT)
        up = jnp.clip(gu[:, D_FF:], -SWIGLU_LIMIT, SWIGLU_LIMIT)
        act = (up + 1.0) * gate * jax.nn.sigmoid(SWIGLU_ALPHA * gate)
        return act @ w_down[e] + b_down[e]

    y = lax.map(expert_block, (x_blocks, block_e)).reshape(cap, d)
    out = jnp.zeros((t + 1, d), hn.dtype).at[tok_buf].add(y * gate_buf[:, None])
    return out[:t].reshape(bsz, length, d)

def setup_inputs(seed: int = 0) -> dict:
    key = jax.random.key(seed)
    ks = jax.random.split(key, 32)
    f32 = jnp.float32
    nrm = lambda k, shape, scale: jax.random.normal(k, shape, f32) * scale
    gain = lambda k, shape: 1.0 + 0.02 * jax.random.normal(k, shape, f32)
    L = DEPTH
    dt0 = jnp.exp(jax.random.uniform(ks[5], (L, DN_HEADS), f32, np.log(1e-3), np.log(1e-1)))
    return {
        'x': nrm(ks[0], (BATCH, SEQ, D_MODEL), 1.0),
        'meta_tokens': nrm(ks[1], (N_META, D_MODEL), 1.0),
        'norm_mix_g': gain(ks[2], (L, D_MODEL)),
        'w_in': nrm(ks[3], (L, D_MODEL, IN_COLS), D_MODEL ** -0.5),
        'conv_qkv_w': nrm(ks[4], (L, SHORT_CONV, 2 * DN_QK + DN_VW), SHORT_CONV ** -0.5),
        'a_log': jnp.log(jax.random.uniform(ks[6], (L, DN_HEADS), f32, 1.0, 16.0)),
        'dt_bias': dt0 + jnp.log(-jnp.expm1(-dt0)),
        'dn_norm_g': gain(ks[7], (L, DN_DV)),
        'w_dn_out': nrm(ks[8], (L, DN_VW, D_MODEL), DN_VW ** -0.5),
        'b_glu': nrm(ks[9], (L, 2 * CONV_CH), 0.02),
        'conv_dw_w': nrm(ks[10], (L, CONV_WIDTH, CONV_CH), CONV_WIDTH ** -0.5),
        'conv_dw_b': nrm(ks[11], (L, CONV_CH), 0.02),
        'conv_ln_g': gain(ks[12], (L, CONV_CH)),
        'conv_ln_b': nrm(ks[13], (L, CONV_CH), 0.02),
        'w_conv_out': nrm(ks[14], (L, CONV_CH, D_MODEL), CONV_CH ** -0.5),
        'b_conv_out': nrm(ks[15], (L, D_MODEL), 0.02),
        'w_merge': nrm(ks[16], (L, D_MODEL, 2 * D_MODEL), D_MODEL ** -0.5),
        'b_merge': nrm(ks[17], (L, 2 * D_MODEL), 0.02),
        'w_out': nrm(ks[18], (L, D_MODEL, D_MODEL), D_MODEL ** -0.5),
        'norm_ffn_g': gain(ks[19], (L, D_MODEL)),
        'w_router': nrm(ks[20], (L, D_MODEL, N_EXPERTS), D_MODEL ** -0.5),
        'b_router': nrm(ks[21], (L, N_EXPERTS), 0.01),
        'w_gate_up': nrm(ks[22], (L, N_EXPERTS, D_MODEL, 2 * D_FF), D_MODEL ** -0.5),
        'b_gate_up': nrm(ks[23], (L, N_EXPERTS, 2 * D_FF), 0.02),
        'w_down': nrm(ks[24], (L, N_EXPERTS, D_FF, D_MODEL), D_FF ** -0.5),
        'b_down': nrm(ks[25], (L, N_EXPERTS, D_MODEL), 0.02),
        'final_norm_g': gain(ks[26], (D_MODEL,)),
    }

def reference(x, meta_tokens, norm_mix_g, w_in, conv_qkv_w, a_log, dt_bias, dn_norm_g,
              w_dn_out, b_glu, conv_dw_w, conv_dw_b, conv_ln_g, conv_ln_b, w_conv_out,
              b_conv_out, w_merge, b_merge, w_out, norm_ffn_g, w_router, b_router,
              w_gate_up, b_gate_up, w_down, b_down, final_norm_g):
    bsz = x.shape[0]
    meta = jnp.broadcast_to(meta_tokens[None].astype(x.dtype), (bsz, N_META, x.shape[-1]))
    h = jnp.concatenate([meta, x], axis=1)
    for l in range(DEPTH):
        hn = rms_norm(h, norm_mix_g[l])
        h = h + mixer_block(hn, w_in[l], conv_qkv_w[l], a_log[l], dt_bias[l], dn_norm_g[l],
                            w_dn_out[l], b_glu[l], conv_dw_w[l], conv_dw_b[l], conv_ln_g[l],
                            conv_ln_b[l], w_conv_out[l], b_conv_out[l], w_merge[l],
                            b_merge[l], w_out[l])
        hn = rms_norm(h, norm_ffn_g[l])
        h = h + moe_ffn(hn, w_router[l], b_router[l], w_gate_up[l], b_gate_up[l],
                        w_down[l], b_down[l])
    out = rms_norm(h, final_norm_g)
    return out[:, N_META:]


_drawn_inputs = setup_inputs


def setup_inputs(seed=0):
    import zlib

    import numpy as np

    out = dict(_drawn_inputs(seed))
    spreads = {}
    factors = {'dn_norm_g': 4.301,
     'b_glu': 3.033,
     'conv_ln_g': 2.762,
     'conv_ln_b': 3.141,
     'b_merge': 5.569,
     'b_router': 2.792,
     'b_gate_up': 5.457,
     'b_down': 6.285,
     'final_norm_g': 7.873,
     'b_conv_out': 6.085}
    for name, (base, spread) in spreads.items():
        noise = np.random.default_rng([zlib.crc32(name.encode()), seed]).standard_normal(out[name].shape)
        drawn = base * np.exp(spread * noise) if base else spread * noise
        out[name] = __import__('jax').numpy.asarray(drawn.astype(out[name].dtype))
    for name, factor in factors.items():
        out[name] = (out[name] * factor).astype(out[name].dtype)
    return out
```

```python
from contextlib import ExitStack

import numpy as np
import concourse.bass as bass
from concourse import mybir

F32 = mybir.dt.float32
I32 = mybir.dt.int32
ACT = mybir.ActivationFunctionType
ALU = mybir.AluOpType
AX = mybir.AxisListType.X

P = 128
D = 1024
KT = D // P
TOK = 256
NT = TOK // P
META = 16
SEQ = META + TOK
H = 4
HW_ = H * P
TAPS = 4
CT = 4
WIDE = 31
PAD = WIDE - 1 - META
E = 32
TOPK = 4
FT = 8
SLOTS = 64
BLOCKS = TOK // SLOTS
EPS = 1e-6
LN_EPS = 1e-5
UNITS = [(META, 0), (P, META), (P, META + P)]

C_TAP = 0
C_BGLU = C_TAP + TAPS * 3 * H
C_DWB = C_BGLU + 2 * CT
C_LNG = C_DWB + CT
C_LNB = C_LNG + CT
C_BCONV = C_LNB + CT
C_BMERGE = C_BCONV + KT
C_NMIX = C_BMERGE + 2 * KT
C_NFFN = C_NMIX + KT
C_DN = C_NFFN + KT
N_COLS = C_DN + 1

Q0, K0, V0 = 0, 4, 8
GB0, GA0, GO0, MG0 = 12, 16, 20, 24
N_PROJ = 40
PROJ_BANKS = 3
TABW = 2 * FT + 2 * NT


def build(nc, x, meta_tokens, norm_mix_g, w_in, conv_qkv_w, a_log, dt_bias, dn_norm_g, w_dn_out,
          b_glu, conv_dw_w, conv_dw_b, conv_ln_g, conv_ln_b, w_conv_out, b_conv_out, w_merge,
          b_merge, w_out, norm_ffn_g, w_router, b_router, w_gate_up, b_gate_up, w_down, b_down,
          final_norm_g, out):
    with ExitStack() as ctx:
        def sb(name, shape, dt=F32):
            return ctx.enter_context(nc.sbuf_tensor(name, shape, dt))

        def sem(name):
            return ctx.enter_context(nc.semaphore(name))

        GU = 2 * FT * P
        ring = sb("ring", [P, 2 * KT * GU + FT * D])
        DN0 = 2 * KT * GU
        gu_w = [[ring[:, (s * KT + k) * GU:(s * KT + k + 1) * GU] for k in range(KT)] for s in range(2)]
        dn_w = [ring[:, DN0 + k * D:DN0 + (k + 1) * D] for k in range(FT)]
        mix_w = [ring[:, DN0 + s * 4 * D:DN0 + (s + 1) * 4 * D] for s in range(2)]

        def carve(base, limit):
            at = [base]

            def take(*shape):
                n = int(np.prod(shape))
                v = area[:, at[0]:at[0] + n]
                at[0] += n
                assert at[0] <= limit
                if len(shape) == 2:
                    return v.rearrange("p (a b) -> p a b", a=shape[0])
                if len(shape) == 3:
                    return v.rearrange("p (a b c) -> p a b c", a=shape[0], b=shape[1])
                return v
            return take

        area = ring
        setA = carve(0, KT * GU)
        qkv = setA(3 * H, SEQ)
        tmpA = setA(H, SEQ)
        tmpB = setA(H, SEQ)
        kbT = setA(H, SEQ)
        growE = setA(H, SEQ)
        gam = setA(3, H, P)
        qkT = setA(2, H, P)
        kB = setA(3, H, P)
        kD = setA(3, H, P)
        vB = setA(3, H, P)
        qdec = setA(2, H, P)
        flatA = ring[:, 3 * H * SEQ:3 * H * SEQ + 2 * H * SEQ]
        nwT = flatA[:, 0:2 * HW_].rearrange("p (u h c) -> p u h c", u=2, h=H)
        vn = flatA[:, 2 * HW_:3 * HW_].rearrange("p (h c) -> p h c", h=H)
        state = flatA[:, 3 * HW_:4 * HW_].rearrange("p (h c) -> p h c", h=H)

        setB = carve(KT * GU, 2 * KT * GU)
        gates = setB(2 * KT, TOK)
        hnT = setB(KT, SEQ)
        sgo = setB(H, TOK)
        uT = setB(CT, PAD + SEQ)
        ucT = setB(CT, TOK)
        oT = setB(H, TOK)
        yT = setB(KT, TOK)
        hn2T = setB(KT, TOK)
        wab = setB(KT, 2 * H)
        wr = setB(KT, E)
        xn = gates[:, 0:8, :].rearrange("p a b -> p (a b)").rearrange("p (t d) -> p t d", t=NT)
        xmn = gates[:, 8:12, :].rearrange("p a b -> p (a b)")
        xm = gates[:, 12:16, :].rearrange("p a b -> p (a b)")
        bgu_rows = yT[:, :, :].rearrange("p a b -> p (a b)")
        rowsA = hn2T[:, 0, 0:P]
        rowsB = hn2T[:, 1, 0:P]
        scr1 = yT[:, 0:4, :]
        scr2 = yT[:, 4:8, :]

        work = sb("work", [P, 7808])
        area = work
        mixW = carve(0, 7808)
        lvl = mixW(7, P)
        aT = mixW(3, H, P)
        inv = mixW(3, H, P)
        invT = mixW(3, H, P)
        xlv = mixW(3, H, P)
        gbc = xlv
        bbc = invT
        t1 = aT[:, 0, :, :].rearrange("p a b -> p (a b)")
        t2 = aT[:, 1, :, :].rearrange("p a b -> p (a b)")
        moeW = carve(0, 7808)
        hN = moeW(NT, D)
        gu_s = moeW(2 * FT * SLOTS)
        tS = moeW(FT, 2, SLOTS)
        sg = moeW(FT, SLOTS)
        hid = moeW(FT, SLOTS)
        xg = moeW(KT, SLOTS)
        y_s = moeW(512)
        moeW(D - 512)
        og = moeW(NT, P)
        pT = moeW(2, TOK)
        oh = moeW(NT, SLOTS)
        hid_end = NT * D + 2 * FT * SLOTS + 2 * FT * SLOTS + 3 * FT * SLOTS
        bd = work[:, hid_end:hid_end + D]
        nov = sg[:, :, :].rearrange("p a b -> p (a b)")[0:E, 0:3 * P].rearrange("p (a c) -> p a c", a=3)
        gT = hid[:, :, :].rearrange("p a b -> p (a b)")[0:E, 0:TOK]
        tS_flat = tS[:, :, :, :].rearrange("p a b c -> p (a b c)")
        xg_o = tS_flat[:, 0:512].rearrange("p (k s) -> p k s", k=KT)
        y_o = gu_s[:, 0:512]
        pT_o = gu_s[:, 512:512 + TOK]
        acc = sb("acc", [P, NT, D])
        ident = sb("ident", [P, P])
        ones = sb("ones", [P, P])
        tri = sb("tri", [P, P])
        tris = sb("tris", [P, P])
        iota = sb("iota", [P, TOK])
        cols = sb("cols", [P, N_COLS])
        dwc = sb("dwc", [P, WIDE * CT])
        tab = sb("tab", [P, E, TABW])
        tabE = sb("tabE", [P, 2, TABW])
        ovi = sb("ovi", [P, 3, E], I32)
        ab = sb("ab", [P, 3, 2 * H])
        tok_s = sb("tok_s", [P, 12, 3, H])
        alog = sb("alog", [P, H])
        dtb = sb("dtb", [P, H])
        brt = sb("brt", [P, E])
        lg = sb("lg", [P, NT, E])
        lg2 = sb("lg2", [P, NT, E])
        msk = sb("msk", [P, NT, E])
        gat = sb("gat", [P, NT, E])
        top = sb("top", [P, NT, 8])
        topi = sb("topi", [P, NT, 8], mybir.dt.uint32)
        topf = sb("topf", [P, NT, 8])
        st = sb("st", [P, 32])
        eps = sb("eps", [P, 2])

        psum = ctx.enter_context(nc.psum_tensor("psum", [P, 8, 512], F32))
        pb = [psum[:, i, :] for i in range(8)]

        def heads(b, n=P, parts=P):
            return pb[b][0:parts, 0:H * n].rearrange("p (h c) -> p h c", h=H)

        s_x, s_meta, s_rows, s_small, s_bd = sem("x_in"), sem("meta_in"), sem("rows_in"), sem("small_in"), sem("bd_in")
        s_bgu, s_wab, s_wr, s_gf = sem("bgu_in"), sem("wab_in"), sem("wr_in"), sem("gf_in")
        s_mixw = [sem("mixw_in0"), sem("mixw_in1")]
        s_gu = [[sem(f"gu_in{s}_{q}") for q in range(KT // 2)] for s in range(2)]
        s_dn = [sem(f"dn_in{k}") for k in range(4)]
        s_out = sem("out_stored")
        s_pool, s_const = sem("pool_step"), sem("consts_made")
        dve, act = sem("dve_step"), sem("act_step")
        s_ptr, s_cols, s_bgutr, s_tab = sem("params_turned"), sem("cols_ready"), sem("bgu_turned"), sem("tab_bias")
        s_ss, s_rt, s_xn = sem("x_squares"), sem("x_root"), sem("x_normed")
        s_ht, s_ha, s_hv = sem("h_turned"), sem("hnT_by_act"), sem("hnT_by_dve")
        s_proj, s_conv, s_gb, s_ga = sem("proj_done"), sem("conv_done"), sem("glu_gate"), sem("glu_out")
        s_gosig, s_go, s_gate = sem("go_sig"), sem("go_out"), sem("merge_gate")
        s_sgq, s_silu, s_sqq = sem("qkv_sig"), sem("qkv_silu"), sem("qk_squares")
        s_l2, s_l2r, s_qkn = sem("l2_sums"), sem("l2_roots"), sem("qk_normed")
        s_abm, s_abv, s_aba = sem("ab_done"), sem("ab_dve"), sem("ab_act")
        s_gbc, s_gr, s_brow, s_bbc = sem("g_bcast"), sem("gcum_rows"), sem("beta_rows"), sem("beta_bcast")
        s_gamx, s_game, s_gamm, s_gre = sem("gamma_diff"), sem("gamma_exp"), sem("gamma_masked"), sem("row_exp")
        s_sm, s_sme, s_smb, s_kb = sem("small_diffs"), sem("small_exps"), sem("small_beta"), sem("kb_ready")
        s_kt, s_ktv, s_kta = sem("kv_turned"), sem("kB_ready"), sem("kDvB_ready")
        s_at, s_atv, s_qd = sem("kk_done"), sem("at_ready"), sem("qdec_ready")
        s_lx, s_lxv, s_ly, s_lyv = sem("lvl_x"), sem("lvl_x_read"), sem("lvl_y"), sem("lvl_y_read")
        s_w, s_wa, s_v0, s_v0a, s_s0, s_s0a = sem("w_done"), sem("nw_ready"), sem("v0"), sem("v0_ready"), sem("s0"), sem("s0_ready")
        s_vn, s_vna, s_o, s_oa, s_su, s_sv = sem("vn"), sem("vn_ready"), sem("o"), sem("oT_ready"), sem("s_upd"), sem("state_ready")
        s_osq, s_on, s_onr, s_og = sem("o_squares"), sem("o_sums"), sem("o_roots"), sem("o_gated")
        s_uc, s_lm, s_lc, s_lsq, s_lv, s_lr = sem("wide_conv"), sem("ln_mean"), sem("ln_centred"), sem("ln_squares"), sem("ln_var"), sem("ln_root")
        s_ln, s_lnz, s_lnsig, s_u2 = sem("ln_scaled"), sem("ln_affine"), sem("ln_sig"), sem("u_ready")
        s_ab2, s_yv, s_wo, s_wov = sem("branches_done"), sem("y_ready"), sem("out_done"), sem("h_ready")
        s_r1, s_r2, s_r3, s_r4, s_r5, s_r6 = sem("r_squares"), sem("r_meansq"), sem("r_root"), sem("r_normed"), sem("r_turned"), sem("hn2T_ready")
        s_lg, s_msk, s_ex, s_gt = sem("logits"), sem("masks_ready"), sem("r_exp"), sem("r_gates")
        s_pos, s_nov, s_ov, s_ovv, s_gtt, s_gtv, s_bm, s_bv = (sem("pos_done"), sem("nov_ready"), sem("ov_done"), sem("tables_ready"),
                                                               sem("gates_turned"), sem("gT_ready"), sem("bias_done"), sem("acc_ready"))
        m_oh, m_ga, m_pt, m_xg, m_ptc = sem("m_onehot"), sem("m_gathered"), sem("m_pt"), sem("m_xg"), sem("m_pt_copied")
        m_gu, m_ea, m_ev, m_t, m_g, m_sig, m_hid = sem("m_gu"), sem("m_gu_act"), sem("m_gu_dve"), sem("m_turned"), sem("m_gate"), sem("m_sig"), sem("m_hidden")
        m_y, m_ye, m_sc, m_add = sem("m_y"), sem("m_y_copied"), sem("m_scattered"), sem("m_added")
        o_pe, o_dve, o_act = sem("further_by_pe"), sem("further_by_dve"), sem("further_by_act")
        s_over = sem("further_blocks_over")
        m_te, m_tb, m_up, m_a = sem("m_staged"), sem("m_biased"), sem("m_up"), sem("m_product")
        s_f1, s_f3, s_f4 = sem("f_squares"), sem("f_root"), sem("f_out")

        MAIN = dict(oh=(m_oh, 4, 0), ga=(m_ga, 1, 0), pt=(m_pt, 1, 0), xg=(m_xg, 1, 0), ptc=(m_ptc, 1, 0), gu=(m_gu, KT // 2, KT // 2 - 1),
                    ea=(m_ea, 1, 0), ev=(m_ev, 1, 0), t=(m_t, 1, 0), tb=(m_tb, 2, 0), g=(m_g, 1, 0), up=(m_up, 1, 0),
                    a=(m_a, 1, 0), sig=(m_sig, 1, 0), hid=(m_hid, 1, 0), y=(m_y, 1, 0), ye=(m_ye, 1, 0), sc=(m_sc, 2, 0),
                    add=(m_add, 2, 0))
        PE_N, DVE_N, ACT_N = 6 + KT // 2, 14, 4
        OVER = dict(ga=(o_pe, PE_N, 0), gu=(o_pe, PE_N, KT // 2), t=(o_pe, PE_N, KT // 2 + 1), pt=(o_pe, PE_N, KT // 2 + 2),
                    y=(o_pe, PE_N, KT // 2 + 3), sc=(o_pe, PE_N, KT // 2 + 4), oh=(o_dve, DVE_N, 0), xg=(o_dve, DVE_N, 4), ev=(o_dve, DVE_N, 5), tb=(o_dve, DVE_N, 6),
                    g=(o_dve, DVE_N, 8), up=(o_dve, DVE_N, 9), a=(o_dve, DVE_N, 10), hid=(o_dve, DVE_N, 11),
                    add=(o_dve, DVE_N, 12), ea=(o_act, ACT_N, 0), ptc=(o_act, ACT_N, 1), sig=(o_act, ACT_N, 2), ye=(o_act, ACT_N, 3))

        def wait(eng, S, step, n, times=1):
            s, by_block, before = S[step]
            eng.wait_ge(s, n * by_block + (before + times))

        N_LVL = 7
        lvl_units = [[u for u in range(3) if (1 << l) < UNITS[u][0]] for l in range(N_LVL)]
        XB = {1: 3, 2: 5, 0: 7}
        YB = {1: 4, 2: 6, 0: 7}

        def l2_root(i):
            return growE[:, i, :] if i < H else tmpB[:, i - H, :]

        def beta_rows(u):
            if u == 0:
                return pb[3][:, H * META:2 * H * META].rearrange("p (h c) -> p h c", h=H)
            return heads(5 + u)

        def small_at(u, what):
            n, _ = UNITS[u]
            b = {"x": XB, "y": YB, "yt": XB}[what][u]
            o = {"x": 0, "y": 64, "yt": 128}[what] if u == 0 else 0
            return pb[b][0:n, o:o + H * n].rearrange("p (h c) -> p h c", h=H)

        def half(m, l, second):
            if len(m.shape) == 2:
                return m.rearrange("p (b t r) -> p b t r", t=2, r=1 << l)[:, :, second, :]
            return m.rearrange("p h (b t r) -> p h b t r", t=2, r=1 << l)[:, :, :, second, :]

        def packed(m, l, n):
            return m[:, :, 0:n // 2].rearrange("p h (b r) -> p h b r", r=1 << l)

        def mix_group(g):
            s = mix_w[g % 2]
            if g < 6:
                c0 = [0, HW_, 2 * HW_, 3 * HW_ + 2 * H + HW_ + 512, 3 * HW_ + 2 * H + HW_, 3 * HW_ + 2 * H][g]
                src = w_in[0][:, c0:c0 + 512].rearrange("(k p) n -> p k n", p=P)
            elif g < 10:
                src = w_merge[0][:, (g - 6) * 512:(g - 5) * 512].rearrange("(k p) n -> p k n", p=P)
            elif g < 12:
                src = (w_dn_out if g == 10 else w_conv_out)[0].rearrange("(k p) n -> p k n", p=P)
                return src, s.rearrange("p (k n) -> p k n", k=4)
            else:
                src = w_out[0][:, (g - 12) * 512:(g - 11) * 512].rearrange("(k p) n -> p k n", p=P)
            return src, s.rearrange("p (k n) -> p k n", k=KT)

        N_MIX = 14

        def wait_mixw(eng, g):
            eng.wait_ge(s_mixw[g % 2], 16 * (g // 2 + 1))

        ROWS = ((C_BGLU, C_DWB, b_glu), (C_DWB, C_LNG, conv_dw_b), (C_LNG, C_LNB, conv_ln_g), (C_LNB, C_BCONV, conv_ln_b),
                (C_BCONV, C_BMERGE, b_conv_out), (C_BMERGE, C_NMIX, b_merge), (C_NMIX, C_NFFN, norm_mix_g),
                (C_NFFN, C_DN, norm_ffn_g), (C_DN, N_COLS, dn_norm_g))

        def rows(eng, dst, src):
            eng.dma_start(dst, src).then_inc(s_rows, 16)

        block = ctx.enter_context(nc.Block())

        @block.sync
        def _(sp):
            def load_gate_up(e, s, q):
                dst = ring[:, (s * KT + 2 * q) * GU:(s * KT + 2 * q + 2) * GU].rearrange("p (k n) -> p k n", k=2)
                src = w_gate_up[0][e].rearrange("(q k p) n -> q p k n", p=P, k=2)[q]
                sp.dma_start(dst, src).then_inc(s_gu[s][q], 16)

            def load_down(e):
                for q in range(4):
                    dst = ring[:, DN0 + 2 * q * D:DN0 + 2 * (q + 1) * D].rearrange("p (k n) -> p k n", k=2)
                    src = w_down[0][e].rearrange("(q k p) n -> q p k n", p=P, k=2)[q]
                    sp.dma_start(dst, src).then_inc(s_dn[q], 16)

            sp.dma_start(acc[:, :, :], x[0].rearrange("(t p) d -> p t d", p=P)).then_inc(s_x, 16)
            for c0, c1, src in ROWS[4:]:
                rows(sp, rowsA[c0:c1, :], src[0].rearrange("(t c) -> t c", c=P))
            rows(sp, rowsB[0:WIDE * CT, :], conv_dw_w[0].rearrange("j (t c) -> (j t) c", c=P))
            for g in range(2):
                src, dst = mix_group(g)
                sp.dma_start(dst, src).then_inc(s_mixw[g % 2], 16)
            sp.dma_start(bgu_rows[0:E, :], b_gate_up[0]).then_inc(s_bgu, 16)
            sp.dma_start(wab, w_in[0][:, 3 * HW_:3 * HW_ + 2 * H].rearrange("(k p) n -> p k n", p=P)).then_inc(s_wab, 16)
            sp.dma_start(alog[:, :], a_log.to_broadcast([P, H])).then_inc(s_small, 16)
            sp.dma_start(dtb[:, :], dt_bias.to_broadcast([P, H])).then_inc(s_small, 16)
            sp.dma_start(brt[:, :], b_router.to_broadcast([P, E])).then_inc(s_small, 16)
            sp.dma_start(wr, w_router[0].rearrange("(k p) n -> p k n", p=P)).then_inc(s_wr, 16)
            for g in range(2, 12):
                sp.wait_ge(s_proj, 4 * (g - 1))
                src, dst = mix_group(g)
                sp.dma_start(dst, src).then_inc(s_mixw[g % 2], 16)
            sp.wait_ge(s_oa, 2)
            sp.dma_start(bd[0:E, :], b_down[0]).then_inc(s_bd, 16)
            for q in (0, 1):
                load_gate_up(0, 0, q)
            for g in (12, 13):
                sp.wait_ge(s_ab2, KT)
                src, dst = mix_group(g)
                sp.dma_start(dst, src).then_inc(s_mixw[g % 2], 16)
            for q in (2, 3):
                load_gate_up(0, 0, q)
            sp.wait_ge(s_yv, KT)
            load_gate_up(1, 1, 0)
            sp.wait_ge(s_wo, 4)
            load_gate_up(1, 1, 1)
            load_gate_up(1, 1, 2)
            load_down(0)
            sp.wait_ge(s_lg, NT)
            load_gate_up(1, 1, 3)

            def load_next(e, s):
                sp.wait_ge(m_gu, (KT // 2) * e + 1)
                sp.sem_inc(s_over, 1)
                more = sp.value_load(ovi[0:1, 0, bass.ds(e, 1)], min_val=0, max_val=BLOCKS - 1)
                last = sp.value_load(ovi[0:1, 2, bass.ds(e, 1)], min_val=0, max_val=E * BLOCKS)
                with sp.If(more > 0):
                    for q in range(KT // 2):
                        sp.wait_ge(o_pe, last * PE_N + (1 + q + 1))
                        sp.sem_inc(s_over, 1)
                        load_gate_up(e + 2, s, q)
                with sp.If(more < 1):
                    for q in range(KT // 2):
                        sp.wait_ge(m_gu, (KT // 2) * e + (q + 1))
                        sp.sem_inc(s_over, 1)
                        load_gate_up(e + 2, s, q)
                sp.wait_ge(m_y, e + 1)
                sp.sem_inc(s_over, 1)
                with sp.If(more > 0):
                    wait(sp, OVER, "y", last)
                    sp.sem_inc(s_over, 1)
                load_down(e + 1)

            sp.wait_ge(s_ovv, 2)
            with sp.Fori(0, E // 2 - 1) as i:
                for s in range(2):
                    load_next(2 * i + s, s)
            sp.wait_ge(m_y, E - 1)
            more = sp.value_load(ovi[0:1, 0, E - 2:E - 1], min_val=0, max_val=BLOCKS - 1)
            with sp.If(more > 0):
                last = sp.value_load(ovi[0:1, 2, E - 2:E - 1], min_val=0, max_val=E * BLOCKS)
                wait(sp, OVER, "y", last)
                sp.sem_inc(s_over, 1)
            load_down(E - 1)
            sp.dma_start(gu_w[0][0][:, 0:D], final_norm_g.rearrange("(a d) -> a d", a=1).to_broadcast([P, D])).then_inc(s_gf, 16)
            for t in range(NT):
                sp.wait_ge(s_f4, t + 1)
                sp.dma_start(out[0][t * P:(t + 1) * P, :], acc[:, t, :]).then_inc(s_out, 16)
            sp.wait_ge(s_out, 16 * NT)

        @block.gpsimd
        def _(pool):
            steps = [0]

            def link(ins):
                steps[0] += 1
                ins.then_inc(s_pool, 1)
                pool.wait_ge(s_pool, steps[0])

            pool.memset(ones[:, :], 1.0).then_inc(s_const, 1)
            pool.memset(eps[:, 0:1], EPS).then_inc(s_const, 1)
            pool.memset(eps[:, 1:2], LN_EPS).then_inc(s_const, 1)
            pool.wait_ge(s_const, 3)
            link(pool.memset(ident[:, :], 0.0))
            pool.affine_select(out=ident[:, :], in_=ident[:, :], compare_op=ALU.not_equal, fill=1.0, base=0,
                               pattern=[[-1, P]], channel_multiplier=1).then_inc(s_const, 1)
            pool.affine_select(out=tri[:, :], in_=ones[:, :], compare_op=ALU.is_ge, fill=0.0, base=0,
                               pattern=[[1, P]], channel_multiplier=-1).then_inc(s_const, 1)
            pool.affine_select(out=tris[:, :], in_=ones[:, :], compare_op=ALU.is_gt, fill=0.0, base=0,
                               pattern=[[1, P]], channel_multiplier=-1).then_inc(s_const, 1)
            link(pool.memset(lvl[:, :, :], 0.0))
            for l in range(N_LVL):
                s = 1 << l
                nb = P // (2 * s)
                v = lvl[:, l, :].rearrange("p (b h r) -> p b h r", h=2, r=s)[:, :, 0, :]
                src = ones[:, 0:P // 2].rearrange("p (b r) -> p b r", r=s)
                link(pool.affine_select(out=v, in_=src, compare_op=ALU.is_ge, fill=0.0, base=-s,
                                        pattern=[[-2 * s, nb], [0, s]], channel_multiplier=1))
                link(pool.affine_select(out=v, in_=v, compare_op=ALU.is_ge, fill=0.0, base=2 * s - 1,
                                        pattern=[[2 * s, nb], [0, s]], channel_multiplier=-1))
            pool.iota(iota[:, :], pattern=[[1, TOK]], base=0, channel_multiplier=0,
                      allow_small_or_imprecise_dtypes=True).then_inc(s_const, 1)

        @block.scalar
        def _(sc):
            steps = [0]

            def step(ins):
                steps[0] += 1
                ins.then_inc(act, 1)

            def settle():
                sc.wait_ge(act, steps[0])

            sc.dma_start(xm[0:META, :], meta_tokens).then_inc(s_meta, 16)
            rows(sc, rowsA[C_TAP:C_BGLU, :], conv_qkv_w[0].rearrange("j (t c) -> (j t) c", c=P))
            for c0, c1, src in ROWS[:4]:
                rows(sc, rowsA[c0:c1, :], src[0].rearrange("(t c) -> t c", c=P))

            sc.wait_ge(s_const, 3)
            nc.scalar.activation(st[:, 30:31], eps[:, 0:1], ACT.Sqrt)
            sc.wait_ge(s_x, 16)
            for t in range(NT):
                nc.scalar.activation(xn[:, t, :], acc[:, t, :], ACT.Square, accum_out=st[:, t:t + 1]).then_inc(s_ss, 1)
            sc.wait_ge(s_meta, 16)
            nc.scalar.activation(xmn[0:META, :], xm[0:META, :], ACT.Square, accum_out=st[0:META, 2:3]).then_inc(s_ss, 1)
            sc.wait_ge(s_ss, 3)
            nc.scalar.activation(st[:, 4:6], st[:, 0:2], ACT.Sqrt, bias=eps[:, 0:1], scale=1.0 / D).then_inc(s_rt, 1)
            nc.scalar.activation(st[0:META, 6:7], st[0:META, 2:3], ACT.Sqrt, bias=eps[0:META, 0:1], scale=1.0 / D).then_inc(s_rt, 1)
            sc.wait_ge(s_cols, 2)
            for k in range(0, KT, 2):
                sc.wait_ge(s_ht, k + 1)
                nc.scalar.activation(hnT[:, k, :], pb[k % 8][:, 0:SEQ], ACT.Copy, scale=cols[:, C_NMIX + k:C_NMIX + k + 1]).then_inc(s_ha, 1)
            for r in range(2):
                sc.wait_ge(s_conv, 4 * (r + 1))
                if r == 1:
                    sc.wait_ge(s_silu, r)
                nc.scalar.activation(tmpA, qkv[:, 4 * r:4 * r + 4, :], ACT.Sigmoid).then_inc(s_sgq, 1)
                sc.wait_ge(s_silu, r + 1)
                if r == 1:
                    sc.wait_ge(s_l2, H)
                nc.scalar.activation(tmpB, qkv[:, 4 * r:4 * r + 4, :], ACT.Square).then_inc(s_sqq, 1)
            for i in range(2 * H):
                sc.wait_ge(s_l2, i + 1)
                nc.scalar.activation(l2_root(i), pb[3 + i % 4][:, 0:SEQ], ACT.Sqrt, bias=eps[:, 0:1]).then_inc(s_l2r, 1)
            sc.wait_ge(s_conv, 12)
            nc.scalar.activation(tmpA, qkv[:, 8:12, :], ACT.Sigmoid).then_inc(s_sgq, 1)
            sc.wait_ge(s_abv, 2)
            nc.scalar.activation(tok_s[:, 2, :, :], tok_s[:, 1, :, :], ACT.Exp, scale=-1.0).then_inc(s_aba, 1)
            nc.scalar.activation(tok_s[:, 4, :, :], ab[:, :, H:2 * H], ACT.Exp, scale=-1.0).then_inc(s_aba, 1)
            sc.wait_ge(s_small, 48)
            nc.scalar.activation(st[:, 8:8 + H], alog[:, :], ACT.Exp).then_inc(s_aba, 1)
            sc.wait_ge(s_aba, 3)
            nc.scalar.activation(tok_s[:, 3, :, :], tok_s[:, 2, :, :], ACT.Ln, bias=ones[:, 0:1]).then_inc(s_aba, 1)
            for i in range(CT):
                sc.wait_ge(s_proj, GB0 + i + 1)
                sc.wait_ge(s_qkn, i + 1)
                nc.scalar.activation(growE[:, i, :], pb[(GB0 + i) % PROJ_BANKS][:, 0:SEQ], ACT.Sigmoid,
                                     bias=cols[:, C_BGLU + CT + i:C_BGLU + CT + i + 1]).then_inc(s_gb, 1)
            for u, (n, c0) in enumerate(UNITS):
                sc.wait_ge(s_gamx, H * (u + 1))
                v = gam[0:n, u, :, 0:n]
                nc.scalar.activation(v, v, ACT.Exp).then_inc(s_game, 1)
                if u == 0:
                    sc.wait_ge(s_ga, CT)
                    continue
                sc.wait_ge(s_sm, u + 1)
                nc.scalar.activation(growE[:, :, c0:c0 + n], heads(3 + u, n), ACT.Exp).then_inc(s_gre, 1)
            sc.wait_ge(s_sm, 3)
            nc.scalar.activation(tok_s[:, 8:10, :, :], tok_s[:, 6:8, :, :], ACT.Exp).then_inc(s_sme, 1)
            sc.wait_ge(s_sme, 1)
            sc.wait_ge(s_smb, 1)
            for u, (n, c0) in enumerate(UNITS):
                sc.wait_ge(s_kt, 2 * u + 2)
                sc.wait_ge(s_ktv, H * (u + 1))
                kb_, vb_ = (3, 4) if u % 2 == 0 else (5, 6)
                for h in range(H):
                    nc.scalar.activation(kD[0:n, u, h, :], heads(kb_, P, n)[:, h, :], ACT.Copy, scale=tok_s[0:n, 9, u, h:h + 1]).then_inc(s_kta, 1)
                    nc.scalar.activation(vB[0:n, u, h, :], heads(vb_, P, n)[:, h, :], ACT.Copy, scale=tok_s[0:n, 5, u, h:h + 1]).then_inc(s_kta, 1)
            for i in range(4):
                sc.wait_ge(s_proj, GO0 + i + 1)
                nc.scalar.activation(scr2[:, i, :], pb[(GO0 + i) % PROJ_BANKS][:, 0:TOK], ACT.Sigmoid).then_inc(s_gosig, 1)
            for i in range(2 * KT):
                sc.wait_ge(s_proj, MG0 + i + 1)
                nc.scalar.activation(gates[:, i, :], pb[(MG0 + i) % PROJ_BANKS][:, 0:TOK], ACT.Sigmoid,
                                     bias=cols[:, C_BMERGE + i:C_BMERGE + i + 1]).then_inc(s_gate, 1)
            for u in (1, 2):
                sc.wait_ge(s_w, u)
                nc.scalar.activation(nwT[:, u - 1, :, :], heads(2 + u), ACT.Copy, scale=-1.0).then_inc(s_wa, 1)
            sc.wait_ge(s_v0, 1)
            nc.scalar.activation(vn[0:META, :, :], heads(5, P, META), ACT.Copy).then_inc(s_v0a, 1)
            sc.wait_ge(s_s0, 1)
            nc.scalar.activation(state[:, :, :], heads(6), ACT.Copy).then_inc(s_s0a, 1)
            for u in (1, 2):
                sc.wait_ge(s_vn, u)
                nc.scalar.activation(vn[:, :, :], heads(7), ACT.Copy).then_inc(s_vna, 1)
                sc.wait_ge(s_o, u)
                nc.scalar.activation(oT[:, :, (u - 1) * P:u * P], heads(3), ACT.Copy).then_inc(s_oa, 1)
            sc.wait_ge(s_oa, 2)
            sc.wait_ge(s_go, 4)
            nc.scalar.activation(scr1, oT, ACT.Square).then_inc(s_osq, 1)
            for c in range(2):
                sc.wait_ge(s_on, c + 1)
                nc.scalar.activation(scr2[:, 2 * c:2 * c + 2, :], pb[3 + c][:, :].rearrange("p (h c) -> p h c", h=2), ACT.Sqrt,
                                     bias=eps[:, 0:1], scale=1.0 / P).then_inc(s_onr, 1)
            sc.wait_ge(s_lc, CT)
            sc.wait_ge(s_on, 2)
            nc.scalar.activation(scr1, ucT, ACT.Square).then_inc(s_lsq, 1)
            sc.wait_ge(s_lv, 1)
            nc.scalar.activation(t1[:, 0:TOK], pb[6][:, 0:TOK], ACT.Sqrt, bias=eps[:, 1:2], scale=1.0 / (CT * P)).then_inc(s_lr, 1)
            sc.wait_ge(s_lnz, CT)
            nc.scalar.activation(scr1, ucT, ACT.Sigmoid).then_inc(s_lnsig, 1)
            sc.wait_ge(s_wov, 4)
            for t in range(NT):
                nc.scalar.activation(hN[:, t, :], acc[:, t, :], ACT.Square, accum_out=st[:, 12 + t:13 + t]).then_inc(s_r1, 1)
            sc.wait_ge(s_r1, 2)
            nc.scalar.activation(st[:, 14:16], st[:, 12:14], ACT.Sqrt, bias=eps[:, 0:1], scale=1.0 / D).then_inc(s_r3, 1)
            for k in range(0, KT, 2):
                sc.wait_ge(s_r5, k + 1)
                nc.scalar.activation(hn2T[:, k, :], pb[k][:, 0:TOK], ACT.Copy, scale=cols[:, C_NFFN + k:C_NFFN + k + 1]).then_inc(s_r6, 1)
            for t in range(NT):
                sc.wait_ge(s_msk, t + 1)
                nc.scalar.activation(gat[:, t, :], lg[:, t, :], ACT.Exp, bias=st[:, 16 + t:17 + t]).then_inc(s_ex, 1)

            def gu_copy(S, n):
                wait(sc, S, "gu", n)
                nc.scalar.activation(gu_s[:, 0:512], pb[0][:, :], ACT.Copy).then_inc(S["ea"][0], 1)

            def pt_copy(S, n, dst):
                wait(sc, S, "pt", n)
                nc.scalar.activation(dst, pb[5][:, 0:TOK], ACT.Copy).then_inc(S["ptc"][0], 1)

            def sigmoid(S, n):
                wait(sc, S, "g", n)
                nc.scalar.activation(sg[:, :, :], tS[:, :, 0, :], ACT.Sigmoid, scale=1.702).then_inc(S["sig"][0], 1)

            def y_copy(S, n, dst):
                wait(sc, S, "y", n)
                nc.scalar.activation(dst, pb[5][:, :], ACT.Copy).then_inc(S["ye"][0], 1)

            def expert(e, j, first, last):
                gu_copy(MAIN, e)
                sigmoid(MAIN, e)
                if not last:
                    pt_copy(MAIN, e + 1, pT[:, 1 - j, :])
                if first:
                    sc.wait_ge(s_bm, 4)
                else:
                    sc.wait_ge(m_sc, 2 * e)
                y_copy(MAIN, e, y_s)
                more = sc.value_load(ovi[0:1, 0, bass.ds(e, 1)], min_val=0, max_val=BLOCKS - 1)
                for b in range(1, BLOCKS):
                    with sc.If(more > b - 1):
                        n = sc.value_load(ovi[0:1, 1, bass.ds(e, 1)], min_val=0, max_val=E * BLOCKS) + (b - 1)
                        gu_copy(OVER, n)
                        pt_copy(OVER, n, pT_o)
                        sigmoid(OVER, n)
                        y_copy(OVER, n, y_o)

            pt_copy(MAIN, 0, pT[:, 0, :])
            sc.wait_ge(s_gtt, 1)
            nc.scalar.activation(gT[:, :], pb[1][0:E, 0:TOK], ACT.Copy).then_inc(s_gtv, 1)
            sc.wait_ge(s_ovv, 2)
            for e in (0, 1):
                expert(e, e, e == 0, False)
            with sc.Fori(1, E // 2 - 1) as i:
                for j in (0, 1):
                    expert(2 * i + j, j, False, False)
            for e in (E - 2, E - 1):
                expert(e, e % 2, False, e == E - 1)
            for t in range(NT):
                sc.wait_ge(m_add, 2 * (E - 1) + 1 + t)
                nc.scalar.activation(hN[:, t, :], acc[:, t, :], ACT.Square, accum_out=st[:, 20 + t:21 + t]).then_inc(s_f1, 1)
            sc.wait_ge(s_f1, 2)
            nc.scalar.activation(st[:, 22:24], st[:, 20:22], ACT.Sqrt, bias=eps[:, 0:1], scale=1.0 / D).then_inc(s_f3, 1)

        @block.tensor
        def _(pe):
            def mm(o, l, r, a=True, z=True, **kw):
                return nc.tensor.matmul(o, l, r, start=a, stop=z, **kw)

            pe.wait_ge(s_const, 4)
            pe.wait_ge(s_rows, 16 * 11)
            nc.tensor.transpose(pb[0][:, 0:N_COLS], rowsA[0:N_COLS, :], ident[0:N_COLS, 0:N_COLS]).then_inc(s_ptr, 1)
            nc.tensor.transpose(pb[1][:, 0:WIDE * CT], rowsB[0:WIDE * CT, :], ident[0:WIDE * CT, 0:WIDE * CT]).then_inc(s_ptr, 1)
            pe.wait_ge(s_cols, 2)
            for k in range(KT):
                if k == 0:
                    pe.wait_ge(s_xn, 3)
                for n, c0 in UNITS:
                    src = xmn[0:META, k * P:(k + 1) * P] if n == META else xn[:, (c0 - META) // P, k * P:(k + 1) * P]
                    last = nc.tensor.transpose(pb[k][:, c0:c0 + n], src, ident[0:n, 0:n])
                last.then_inc(s_ht, 1)
            pe.wait_ge(s_ha, KT // 2)
            pe.wait_ge(s_hv, KT // 2)

            def freed(i):
                for first, s in ((MG0, s_gate), (GO0, s_go), (GA0, s_ga), (GB0, s_gb), (0, s_conv)):
                    if i >= first:
                        pe.wait_ge(s, i - first + 1)
                        return

            def project(i):
                if i >= PROJ_BANKS:
                    freed(i - PROJ_BANKS)
                g = i // 4
                wait_mixw(pe, g)
                _, w = mix_group(g)
                c0 = META if i >= GO0 else 0
                for k in range(KT):
                    last = mm(pb[i % PROJ_BANKS][:, 0:SEQ - c0], w[:, k, (i % 4) * P:(i % 4 + 1) * P], hnT[:, k, c0:SEQ],
                              k == 0, k == KT - 1)
                last.then_inc(s_proj, 1)

            def l2_sum(i):
                if i >= 4:
                    pe.wait_ge(s_l2r, i - 3)
                mm(pb[3 + i % 4][:, 0:SEQ], ones[:, :], tmpB[:, i % H, :]).then_inc(s_l2, 1)

            for i in range(K0):
                project(i)
            pe.wait_ge(s_bgu, 16)
            for f in range(2 * FT):
                last = nc.tensor.transpose(pb[7][:, f * E:(f + 1) * E], bgu_rows[0:E, f * P:(f + 1) * P], ident[0:E, 0:E])
            last.then_inc(s_bgutr, 1)
            for i in range(K0, V0):
                project(i)
            pe.wait_ge(s_sqq, 1)
            for i in range(H):
                l2_sum(i)
            for i in range(V0, GB0):
                project(i)
                if i == GB0 - 2:
                    pe.wait_ge(s_sqq, 2)
                    for h in range(H, 2 * H):
                        l2_sum(h)
            pe.wait_ge(s_wab, 16)
            pe.wait_ge(s_tab, 2)
            for u, (n, c0) in enumerate(UNITS):
                for k in range(KT):
                    last = mm(pb[7][0:n, 2 * H * u:2 * H * (u + 1)], hnT[:, k, c0:c0 + n], wab[:, k, :], k == 0, k == KT - 1)
                last.then_inc(s_abm, 1)
            for i in range(GB0, GO0):
                project(i)
            pe.wait_ge(s_const, 6)
            pe.wait_ge(s_l2r, 2 * H)
            for u, (n, c0) in enumerate(UNITS):
                pe.wait_ge(s_gbc, u + 1)
                for h in range(H):
                    last = mm(heads(3 + u, n)[:, h, :], gbc[0:n, u, h, :], tri[0:n, 0:n])
                last.then_inc(s_gr, 1)
            for u, (n, c0) in enumerate(UNITS):
                pe.wait_ge(s_bbc, u + 1)
                for h in range(H):
                    last = mm(beta_rows(u)[:, h, :], bbc[0:n, u, h, :], ident[0:n, 0:n])
                last.then_inc(s_brow, 1)
            project(GO0)
            pe.wait_ge(s_sm, 3)
            pe.wait_ge(s_gre, 2)
            pe.wait_ge(s_kb, 3)
            for u, (n, c0) in enumerate(UNITS):
                kb_, vb_ = (3, 4) if u % 2 == 0 else (5, 6)
                if u == 2:
                    pe.wait_ge(s_ktv, 4)
                    pe.wait_ge(s_kta, 8)
                for base, b in ((K0, kb_), (V0, vb_)):
                    for h in range(H):
                        last = nc.tensor.transpose(heads(b, P, n)[:, h, :], qkv[:, base + h, c0:c0 + n], ident[:, :])
                    last.then_inc(s_kt, 1)
            project(GO0 + 1)
            for u, (n, c0) in enumerate(UNITS):
                if u == 0:
                    pe.wait_ge(s_ktv, 12)
                    pe.wait_ge(s_kta, 24)
                for h in range(H):
                    last = mm(heads(3 + u, n, n)[:, h, :], qkv[:, K0 + h, c0:c0 + n], kbT[:, h, c0:c0 + n])
                last.then_inc(s_at, 1)
            for u in (1, 2):
                n, c0 = UNITS[u]
                for h in range(H):
                    last = mm(heads(5 + u)[:, h, :], qkv[:, K0 + h, c0:c0 + n], qkv[:, Q0 + h, c0:c0 + n])
                last.then_inc(s_at, 1)
            project(GO0 + 2)
            nxt = [GO0 + 3]

            def fill(count):
                for _ in range(count):
                    if nxt[0] < N_PROJ:
                        project(nxt[0])
                        nxt[0] += 1

            pe.wait_ge(s_atv, 5)
            nx = 0
            solved = 3
            for l in range(N_LVL):
                pe.wait_ge(s_lyv, solved)
                for u in lvl_units[l]:
                    n, _ = UNITS[u]
                    for h in range(H):
                        last = mm(small_at(u, "x")[:, h, 0:n // 2], aT[0:n, u, h, 0:n], half(inv[0:n, u, h, 0:n], l, 0))
                    last.then_inc(s_lx, 1)
                fill(1)
                for u in lvl_units[l]:
                    n, _ = UNITS[u]
                    nx += 1
                    pe.wait_ge(s_lxv, nx)
                    if 4 << l <= n:
                        for h in range(H):
                            mm(small_at(u, "y")[:, h, 0:n // 2], invT[0:n, u, h, 0:n], half(xlv[0:n, u, h, 0:n], l, 0))
                    for h in range(H):
                        last = mm(small_at(u, "yt")[:, h, 0:n // 2], xlv[0:n, u, h, 0:n], half(invT[0:n, u, h, 0:n], l, 1))
                    last.then_inc(s_ly, 1)
                solved += len(lvl_units[l])
                fill(1 + l % 2)
            fill(N_PROJ)
            pe.wait_ge(s_lyv, solved)
            for u in (1, 2):
                for h in range(H):
                    last = mm(heads(2 + u)[:, h, :], kB[:, u, h, :], invT[:, u, h, :])
                last.then_inc(s_w, 1)
            for h in range(H):
                last = mm(heads(5, P, META)[:, h, :], invT[0:META, 0, h, 0:META], vB[0:META, 0, h, :])
            last.then_inc(s_v0, 1)
            pe.wait_ge(s_v0a, 1)
            for h in range(H):
                last = mm(heads(6)[:, h, :], kD[0:META, 0, h, :], vn[0:META, h, :])
            last.then_inc(s_s0, 1)
            pe.wait_ge(s_qd, 2)
            pe.wait_ge(s_wa, 2)
            for u in (1, 2):
                if u == 1:
                    pe.wait_ge(s_s0a, 1)
                else:
                    pe.wait_ge(s_sv, H)
                for h in range(H):
                    mm(heads(7)[:, h, :], invT[:, u, h, :], vB[:, u, h, :], True, False)
                    last = mm(heads(7)[:, h, :], nwT[:, u - 1, h, :], state[:, h, :], False, True)
                last.then_inc(s_vn, 1)
                pe.wait_ge(s_vna, u)
                if u == 2:
                    pe.wait_ge(s_oa, 1)
                for h in range(H):
                    mm(heads(3)[:, h, :], state[:, h, :], qdec[:, u - 1, h, :], True, False)
                    last = mm(heads(3)[:, h, :], vn[:, h, :], qkT[:, u - 1, h, :], False, True)
                last.then_inc(s_o, 1)
                if u == 1:
                    for h in range(H):
                        last = mm(heads(4)[:, h, :], kD[:, u, h, :], vn[:, h, :])
                    last.then_inc(s_su, 1)
            pe.wait_ge(s_uc, CT)
            for c in range(CT):
                last = mm(pb[5][:, 0:TOK], ones[:, :], ucT[:, c, :], c == 0, c == CT - 1)
            last.then_inc(s_lm, 1)
            pe.wait_ge(s_osq, 1)
            pe.wait_ge(s_sv, H)
            for c in range(2):
                mm(pb[3 + c][:, :].rearrange("p (h c) -> p h c", h=2), ones[:, :], scr1[:, 2 * c:2 * c + 2, :]).then_inc(s_on, 1)
            pe.wait_ge(s_lsq, 1)
            for c in range(CT):
                last = mm(pb[6][:, 0:TOK], ones[:, :], scr1[:, c, :], c == 0, c == CT - 1)
            last.then_inc(s_lv, 1)
            pe.wait_ge(s_og, 1)
            wait_mixw(pe, 10)
            wait_mixw(pe, 11)
            _, wd = mix_group(10)
            _, wc = mix_group(11)
            pe.wait_ge(s_gate, 2 * KT)
            for m in range(KT):
                if m >= 2:
                    pe.wait_ge(s_yv, m - 1)
                for c in range(4):
                    mm(pb[m % 2][:, 0:TOK], wd[:, c, m * P:(m + 1) * P], oT[:, c, :], c == 0, c == 3)
                if m == 0:
                    pe.wait_ge(s_u2, 1)
                for c in range(4):
                    last = mm(pb[6 + m % 2][:, 0:TOK], wc[:, c, m * P:(m + 1) * P], ucT[:, c, :], c == 0, c == 3)
                last.then_inc(s_ab2, 1)
            for c in range(2):
                wait_mixw(pe, 12 + c)
                _, w = mix_group(12 + c)
                for t in range(NT):
                    for k in range(KT):
                        if c == 0 and t == 0:
                            pe.wait_ge(s_yv, k + 1)
                        last = mm(pb[2 + 2 * c + t][:, :], yT[:, k, t * P:(t + 1) * P], w[:, k, :], k == 0, k == KT - 1)
                    last.then_inc(s_wo, 1)
            pe.wait_ge(s_r4, 2)
            for k in range(KT):
                for t in range(NT):
                    last = nc.tensor.transpose(pb[k][:, t * P:(t + 1) * P], hN[:, t, k * P:(k + 1) * P], ident[:, :])
                last.then_inc(s_r5, 1)
            pe.wait_ge(s_wr, 16)
            pe.wait_ge(s_r6, KT // 2)
            pe.wait_ge(s_hv, KT)
            for t in range(NT):
                for k in range(KT):
                    last = mm(pb[t][:, 0:E], hn2T[:, k, t * P:(t + 1) * P], wr[:, k, :], k == 0, k == KT - 1)
                last.then_inc(s_lg, 1)
            pe.wait_ge(s_msk, 4)
            mm(pb[2][:, 0:E], tris[:, :], msk[:, 0, :])
            mm(pb[2][:, E:2 * E], tris[:, :], msk[:, 1, :], True, False)
            mm(pb[2][:, E:2 * E], ones[:, :], msk[:, 0, :], False, True).then_inc(s_pos, 1)
            for t in range(NT):
                last = mm(pb[3][0:E, 0:P], msk[:, t, :], ones[:, :], t == 0, t == NT - 1)
            last.then_inc(s_pos, 1)
            def gather(S, n):
                wait(pe, S, "oh", n, 2 * NT)
                for k in range(KT):
                    for t in range(NT):
                        last = mm(pb[4][:, k * SLOTS:(k + 1) * SLOTS], hN[:, t, k * P:(k + 1) * P], oh[:, t, :], t == 0, t == NT - 1)
                last.then_inc(S["ga"][0], 1)

            def turn_pt(S, n):
                for t in range(NT):
                    last = nc.tensor.transpose(pb[5][:, t * P:(t + 1) * P], og[:, t, :], ident[:, :])
                last.then_inc(S["pt"][0], 1)

            def gate_up(S, n, j, src, arrived):
                wait(pe, S, "xg", n)
                for k in range(KT):
                    if arrived is not None and k % 2 == 0:
                        pe.wait_ge(s_gu[j][k // 2], arrived)
                    for c in range(2):
                        mm(pb[c][0:SLOTS, :], src[:, k, :], gu_w[j][k][:, c * 512:(c + 1) * 512], k == 0, k == KT - 1)
                        last = mm(pb[c][SLOTS:P, :], src[:, k, :], gu_w[j][k][:, D + c * 512:D + (c + 1) * 512], k == 0, k == KT - 1)
                    if k % 2:
                        last.then_inc(S["gu"][0], 1)

            def turn_gu(S, n):
                wait(pe, S, "ea", n)
                wait(pe, S, "ev", n)
                for f in range(FT):
                    last = nc.tensor.transpose(pb[2 + f // 4][:, (f % 4) * P:(f % 4 + 1) * P], gu_s[:, f * P:(f + 1) * P], ident[:, :])
                last.then_inc(S["t"][0], 1)

            def down(S, n, arrived):
                wait(pe, S, "hid", n)
                for f in range(FT):
                    if arrived is not None and f % 2 == 0:
                        pe.wait_ge(s_dn[f // 2], arrived)
                    for c in range(2):
                        last = mm(pb[5][c * SLOTS:(c + 1) * SLOTS, :], hid[:, f, :], dn_w[f][:, c * 512:(c + 1) * 512], f == 0, f == FT - 1)
                last.then_inc(S["y"][0], 1)

            def scatter(S, n, t, w, y):
                for c in range(2):
                    r = slice(c * SLOTS, (c + 1) * SLOTS)
                    last = mm(pb[6 + c][:, :], w[r, t * P:(t + 1) * P], y[r, :])
                last.then_inc(S["sc"][0], 1)

            def output_biases():
                pe.wait_ge(s_ovv, 2)
                pe.wait_ge(s_bd, 16)
                for t in range(NT):
                    for c in range(2):
                        if t == 1:
                            pe.wait_ge(s_bv, c + 1)
                        mm(pb[6 + c][:, :], gT[:, t * P:(t + 1) * P], bd[0:E, c * 512:(c + 1) * 512]).then_inc(s_bm, 1)

            def expert(e, i, j, first, second, last_e):
                gate_up(MAIN, e, j, xg, 16 * (i + 1))
                if first:
                    output_biases()
                else:
                    pe.wait_ge(m_ye, e)
                    if second:
                        pe.wait_ge(s_bv, 4)
                    else:
                        pe.wait_ge(m_add, 2 * e - 2)
                    scatter(MAIN, e - 1, 0, pT[:, 1 - j, :], y_s)
                turn_gu(MAIN, e)
                if not last_e:
                    gather(MAIN, e + 1)
                if not first:
                    pe.wait_ge(m_add, 2 * e - 1)
                    scatter(MAIN, e - 1, 1, pT[:, 1 - j, :], y_s)
                if not last_e:
                    turn_pt(MAIN, e + 1)
                    pe.wait_ge(m_ptc, e + 2)
                down(MAIN, e, 16 * (e + 1))
                more = pe.value_load(ovi[0:1, 0, bass.ds(e, 1)], min_val=0, max_val=BLOCKS - 1)
                for b in range(1, BLOCKS):
                    with pe.If(more > b - 1):
                        n = pe.value_load(ovi[0:1, 1, bass.ds(e, 1)], min_val=0, max_val=E * BLOCKS) + (b - 1)
                        gather(OVER, n)
                        gate_up(OVER, n, j, xg_o, None)
                        turn_gu(OVER, n)
                        pe.wait_ge(m_ye, e + 1)
                        turn_pt(OVER, n)
                        wait(pe, OVER, "ptc", n)
                        down(OVER, n, None)
                        wait(pe, OVER, "ye", n)
                        if first:
                            pe.wait_ge(s_bv, 4)
                        else:
                            pe.wait_ge(m_add, 2 * e)
                        scatter(OVER, n, 0, pT_o, y_o)
                        wait(pe, OVER, "add", n, 1)
                        scatter(OVER, n, 1, pT_o, y_o)
                        wait(pe, OVER, "add", n, 2)
            gather(MAIN, 0)
            turn_pt(MAIN, 0)
            for t in range(NT):
                last = nc.tensor.transpose(pb[1][0:E, t * P:(t + 1) * P], gat[:, t, :], ident[:, :])
            last.then_inc(s_gtt, 1)
            pe.wait_ge(s_nov, 1)
            mm(pb[6][:, 0:E], nov[:, 2, :], ident[0:E, 0:E])
            mm(pb[6][:, E:2 * E], nov[:, 2, :], tris[0:E, 0:E])
            mm(pb[6][:, 2 * E:3 * E], nov[:, 2, :], tri[0:E, 0:E]).then_inc(s_ov, 1)
            pe.wait_ge(s_gtv, 1)
            pe.wait_ge(m_ptc, 1)
            for e in (0, 1):
                expert(e, 0, e, e == 0, e == 1, False)
            with pe.Fori(1, E // 2 - 1) as i:
                for j in (0, 1):
                    expert(2 * i + j, i, j, False, False, False)
            for e in (E - 2, E - 1):
                expert(e, e // 2, e % 2, False, False, e == E - 1)
            pe.wait_ge(m_ye, E)
            for t in range(NT):
                pe.wait_ge(m_add, 2 * (E - 1) + t)
                scatter(MAIN, E - 1, t, pT[:, 1, :], y_s)

        @block.vector
        def _(v):
            steps = [0]

            def step(ins):
                steps[0] += 1
                ins.then_inc(dve, 1)

            def settle():
                v.wait_ge(dve, steps[0])

            V = nc.vector
            step(V.memset(uT[:, :, 0:PAD], 0.0))
            step(V.memset(ab[:, :, :], 0.0))
            step(V.memset(tok_s[:, :, :, :], 0.0))
            v.wait_ge(s_ptr, 1)
            V.tensor_copy(cols[:, :], pb[0][:, 0:N_COLS]).then_inc(s_cols, 1)
            v.wait_ge(s_ptr, 2)
            V.tensor_copy(dwc[:, :], pb[1][:, 0:WIDE * CT]).then_inc(s_cols, 1)
            v.wait_ge(s_rt, 2)
            step(V.reciprocal(st[:, 4:6], st[:, 4:6]))
            step(V.reciprocal(st[0:META, 6:7], st[0:META, 6:7]))
            settle()
            for t in range(NT):
                V.tensor_scalar(xn[:, t, :], acc[:, t, :], st[:, 4 + t:5 + t], None, ALU.mult).then_inc(s_xn, 1)
            V.tensor_scalar(xmn[0:META, :], xm[0:META, :], st[0:META, 6:7], None, ALU.mult).then_inc(s_xn, 1)
            v.wait_ge(s_cols, 2)
            for k in range(1, KT, 2):
                v.wait_ge(s_ht, k + 1)
                V.tensor_scalar(hnT[:, k, :], pb[k % 8][:, 0:SEQ], cols[:, C_NMIX + k:C_NMIX + k + 1], None, ALU.mult).then_inc(s_hv, 1)

            def short_conv(i):
                v.wait_ge(s_proj, i + 1)
                src = pb[i % PROJ_BANKS]
                dst = qkv[:, i, :]
                tap = lambda j: cols[:, C_TAP + j * 3 * H + i:C_TAP + j * 3 * H + i + 1]
                step(V.tensor_scalar(dst, src[:, 0:SEQ], tap(TAPS - 1), None, ALU.mult))
                for s in range(1, TAPS):
                    settle()
                    ins = V.scalar_tensor_tensor(out=dst[:, s:SEQ], in0=src[:, 0:SEQ - s], scalar=tap(TAPS - 1 - s), in1=dst[:, s:SEQ],
                                                 op0=ALU.mult, op1=ALU.add)
                    if s < TAPS - 1:
                        step(ins)
                    else:
                        ins.then_inc(s_conv, 1)

            def silu(r):
                v.wait_ge(s_sgq, r + 1)
                v.wait_ge(s_conv, 4 * r + 4)
                V.tensor_tensor(qkv[:, 4 * r:4 * r + 4, :], qkv[:, 4 * r:4 * r + 4, :], tmpA, ALU.mult).then_inc(s_silu, 1)

            def l2_norm(i):
                v.wait_ge(s_l2r, i + 1)
                root, r = l2_root(i), qkv[:, i, :]
                step(V.reciprocal(root, root))
                settle()
                if i < H:
                    V.scalar_tensor_tensor(out=r, in0=r, scalar=float(P) ** -0.5, in1=root, op0=ALU.mult, op1=ALU.mult).then_inc(s_qkn, 1)
                else:
                    V.tensor_tensor(r, r, root, ALU.mult).then_inc(s_qkn, 1)

            z, az, ez, lz, eb, bt, gc, kd, eg, ekd, g_, bg = (tok_s[:, i, :, :] for i in range(12))

            def decay_and_beta():
                v.wait_ge(s_aba, 4)
                v.wait_ge(s_abv, 2)
                step(V.tensor_tensor(g_, z, lz, ALU.add))
                step(V.tensor_scalar(eb, eb, 1.0, None, ALU.add))
                settle()
                step(V.reciprocal(bt, eb))
                for u in range(3):
                    step(V.scalar_tensor_tensor(out=g_[:, u, :], in0=g_[:, u, :], scalar=-1.0, in1=st[:, 8:8 + H], op0=ALU.mult, op1=ALU.mult))
                settle()
                for u, (n, c0) in enumerate(UNITS):
                    V.tensor_copy(gbc[0:n, u, :, :], g_[0:n, u, :].unsqueeze(2).to_broadcast([n, H, P])).then_inc(s_gbc, 1)
                for u, (n, c0) in enumerate(UNITS):
                    V.tensor_copy(bbc[0:n, u, :, :], bt[0:n, u, :].unsqueeze(2).to_broadcast([n, H, P])).then_inc(s_bbc, 1)

            for i in range(4):
                short_conv(i)
            v.wait_ge(s_bgutr, 1)
            for g in range(2):
                V.tensor_copy(tab[:, :, g:2 * FT:2],
                              pb[7][:, g * FT * E:(g + 1) * FT * E].rearrange("p (f e) -> p e f", f=FT)).then_inc(s_tab, 1)
            silu(0)
            for i in range(4, 8):
                short_conv(i)
            silu(1)
            for i in range(8, 12):
                short_conv(i)
                if i in (9, 10):
                    l2_norm(i - 9)
            silu(2)
            v.wait_ge(s_abm, 3)
            v.wait_ge(s_small, 48)
            settle()
            for u, (n, c0) in enumerate(UNITS):
                step(V.tensor_copy(ab[0:n, u, :], pb[7][0:n, 2 * H * u:2 * H * (u + 1)]))
            settle()
            for u in range(3):
                last = V.tensor_tensor(z[:, u, :], ab[:, u, 0:H], dtb[:, :], ALU.add)
                step(last)
            settle()
            V.scalar_tensor_tensor(out=az, in0=z, scalar=-1.0, in1=z, op0=ALU.mult, op1=ALU.max).then_inc(s_abv, 1)
            V.tensor_scalar(z, z, 0.0, None, ALU.max).then_inc(s_abv, 1)
            for i in range(2, 2 * H):
                l2_norm(i)
            decay_and_beta()
            for i in range(CT):
                v.wait_ge(s_proj, GA0 + i + 1)
                v.wait_ge(s_gb, i + 1)
                V.scalar_tensor_tensor(out=uT[:, i, PAD:PAD + SEQ], in0=pb[(GA0 + i) % PROJ_BANKS][:, 0:SEQ],
                                       scalar=cols[:, C_BGLU + i:C_BGLU + i + 1], in1=growE[:, i, :],
                                       op0=ALU.add, op1=ALU.mult).then_inc(s_ga, 1)
            for u, (n, c0) in enumerate(UNITS):
                v.wait_ge(s_gr, u + 1)
                if u == 0:
                    v.wait_ge(s_brow, 1)
                gr = heads(3 + u, n)
                for h in range(H):
                    step(V.tensor_tensor_reduce(out=gam[0:n, u, h, 0:n], in0=gr[0:n, h, :], in1=ident[0:n, 0:n], scale=1.0, scalar=0.0,
                                                op0=ALU.mult, op1=ALU.add, accum_out=gc[0:n, u, h:h + 1]))
                settle()
                for h in range(H):
                    V.tensor_scalar(gam[0:n, u, h, 0:n], gr[0:n, h, :], gc[0:n, u, h:h + 1], 0.0, ALU.subtract, ALU.min).then_inc(s_gamx, 1)
                V.tensor_tensor(kd[0:n, u, :], gr[0:n, :, n - 1], gc[0:n, u, :], ALU.subtract).then_inc(s_sm, 1)
            for u, (n, c0) in enumerate(UNITS):
                v.wait_ge(s_brow, u + 1)
                if u == 0:
                    v.wait_ge(s_qkn, 2 * H)
                V.tensor_tensor(kbT[:, :, c0:c0 + n], beta_rows(u), qkv[:, K0:K0 + H, c0:c0 + n], ALU.mult).then_inc(s_kb, 1)
            v.wait_ge(s_sme, 1)
            V.tensor_tensor(bg, bt, eg, ALU.mult).then_inc(s_smb, 1)
            v.wait_ge(s_smb, 1)
            for u, (n, c0) in enumerate(UNITS):
                v.wait_ge(s_game, u + 1)
                g3 = gam[0:n, u, :, 0:n]
                V.tensor_tensor(g3, g3, tri[0:n, 0:n].unsqueeze(1).to_broadcast([n, H, n]), ALU.mult).then_inc(s_gamm, 1)
            for u, (n, c0) in enumerate(UNITS):
                i3 = ident[0:n, 0:n].unsqueeze(1).to_broadcast([n, H, n])
                step(V.tensor_copy(inv[0:n, u, :, 0:n], i3))
                V.tensor_copy(invT[0:n, u, :, 0:n], i3).then_inc(s_lyv, 1)
            for u, (n, c0) in enumerate(UNITS):
                v.wait_ge(s_kt, 2 * u + 1)
                kb_ = 3 if u % 2 == 0 else 5
                for h in range(H):
                    V.tensor_scalar(kB[0:n, u, h, :], heads(kb_, P, n)[:, h, :], bg[0:n, u, h:h + 1], None, ALU.mult).then_inc(s_ktv, 1)
            v.wait_ge(s_gre, 2)
            for u in (1, 2):
                n, c0 = UNITS[u]
                V.tensor_tensor(qdec[:, u - 1, :, :], qkv[:, 0:H, c0:c0 + n], growE[:, :, c0:c0 + n], ALU.mult).then_inc(s_qd, 1)

            def go(i):
                v.wait_ge(s_gosig, i + 1)
                V.tensor_tensor(sgo[:, i, :], pb[(GO0 + i) % PROJ_BANKS][:, 0:TOK], scr2[:, i, :], ALU.mult).then_inc(s_go, 1)

            v.wait_ge(s_gamm, 3)
            for u, (n, c0) in enumerate(UNITS):
                v.wait_ge(s_at, u + 1)
                V.tensor_tensor(aT[0:n, u, :, 0:n], heads(3 + u, n, n), gam[0:n, u, :, 0:n], ALU.mult).then_inc(s_atv, 1)
            for u in (1, 2):
                v.wait_ge(s_at, 3 + u)
                V.tensor_tensor(qkT[:, u - 1, :, :], heads(5 + u), gam[:, u, :, :], ALU.mult).then_inc(s_atv, 1)
            go(0)
            go(1)
            go(2)
            settle()
            v.wait_ge(s_lyv, 3)
            v.wait_ge(s_pool, 2 + 2 * N_LVL)

            tapat = [0]

            def wide_taps(count):
                for _ in range(count):
                    j = tapat[0]
                    if j == WIDE:
                        return
                    tapat[0] += 1
                    if j:
                        settle()
                    else:
                        v.wait_ge(s_ga, CT)
                    for c in range(CT):
                        w = dwc[:, j * CT + c:j * CT + c + 1]
                        src = uT[:, c, j:j + TOK]
                        if j == 0:
                            ins = V.tensor_scalar(ucT[:, c, :], src, w, cols[:, C_DWB + c:C_DWB + c + 1], ALU.mult, ALU.add)
                        else:
                            ins = V.scalar_tensor_tensor(out=ucT[:, c, :], in0=src, scalar=w, in1=ucT[:, c, :], op0=ALU.mult, op1=ALU.add)
                        if j == WIDE - 1:
                            ins.then_inc(s_uc, 1)
                        else:
                            step(ins)

            for u, (n, c0) in enumerate(UNITS):
                step(V.memset(half(xlv[0:n, u, :, 0:n], 0, 1), 0.0))
            nx = ny = 0
            for l in range(N_LVL):
                settle()
                for u in lvl_units[l]:
                    n, _ = UNITS[u]
                    nx += 1
                    v.wait_ge(s_lx, nx)
                    V.tensor_tensor(half(xlv[0:n, u, :, 0:n], l, 0), packed(small_at(u, "x"), l, n),
                                    half(lvl[0:n, l, 0:n], l, 0).unsqueeze(1).to_broadcast([n, H, n >> (l + 1), 1 << l]), ALU.mult).then_inc(s_lxv, 1)
                wide_taps(2)
                for u in lvl_units[l]:
                    n, _ = UNITS[u]
                    ny += 1
                    v.wait_ge(s_ly, ny)
                    if 4 << l <= n:
                        a = half(inv[0:n, u, :, 0:n], l, 0)
                        step(V.tensor_tensor(a, a, packed(small_at(u, "y"), l, n), ALU.subtract))
                        settle()
                    a = half(invT[0:n, u, :, 0:n], l, 1)
                    V.tensor_tensor(a, a, packed(small_at(u, "yt"), l, n), ALU.subtract).then_inc(s_lyv, 1)
                    if 4 << l <= n:
                        step(V.memset(half(xlv[0:n, u, :, 0:n], l + 1, 1), 0.0))
                if l == 0:
                    go(3)
                wide_taps(3)
            wide_taps(WIDE)
            v.wait_ge(s_su, 1)
            v.wait_ge(s_s0a, 1)
            c1 = META + P - 1
            v.wait_ge(s_o, 1)
            for h in range(H):
                V.scalar_tensor_tensor(out=state[:, h, :], in0=state[:, h, :], scalar=growE[:, h, c1:c1 + 1], in1=heads(4)[:, h, :],
                                       op0=ALU.mult, op1=ALU.add).then_inc(s_sv, 1)
            v.wait_ge(s_lm, 1)
            for c in range(CT):
                V.scalar_tensor_tensor(out=ucT[:, c, :], in0=pb[5][:, 0:TOK], scalar=-1.0 / (CT * P), in1=ucT[:, c, :],
                                       op0=ALU.mult, op1=ALU.add).then_inc(s_lc, 1)
            v.wait_ge(s_onr, 2)
            step(V.reciprocal(scr2, scr2))
            settle()
            step(V.scalar_tensor_tensor(out=oT[:, :, :], in0=oT[:, :, :], scalar=cols[:, C_DN:C_DN + 1], in1=sgo[:, :, :], op0=ALU.mult, op1=ALU.mult))
            settle()
            V.tensor_tensor(oT[:, :, :], oT[:, :, :], scr2, ALU.mult).then_inc(s_og, 1)
            v.wait_ge(s_lr, 1)
            step(V.reciprocal(t1[:, 0:TOK], t1[:, 0:TOK]))
            settle()
            v.wait_ge(s_lc, CT)
            for c in range(CT):
                V.tensor_tensor(ucT[:, c, :], ucT[:, c, :], t1[:, 0:TOK], ALU.mult).then_inc(s_ln, 1)
            v.wait_ge(s_ln, CT)
            for c in range(CT):
                V.tensor_scalar(ucT[:, c, :], ucT[:, c, :], cols[:, C_LNG + c:C_LNG + c + 1], cols[:, C_LNB + c:C_LNB + c + 1],
                                ALU.mult, ALU.add).then_inc(s_lnz, 1)
            v.wait_ge(s_lnsig, 1)
            V.tensor_tensor(ucT[:, :, :], ucT[:, :, :], scr1, ALU.mult).then_inc(s_u2, 1)
            v.wait_ge(s_gate, 2 * KT)
            v.wait_ge(s_u2, 1)
            for m in range(KT):
                v.wait_ge(s_ab2, m + 1)
                a, b = t1[:, (m % 2) * TOK:(m % 2 + 1) * TOK], t2[:, (m % 2) * TOK:(m % 2 + 1) * TOK]
                step(V.tensor_tensor(a, pb[m % 2][:, 0:TOK], gates[:, m, :], ALU.mult))
                step(V.scalar_tensor_tensor(out=b, in0=pb[6 + m % 2][:, 0:TOK], scalar=cols[:, C_BCONV + m:C_BCONV + m + 1],
                                            in1=gates[:, KT + m, :], op0=ALU.add, op1=ALU.mult))
                settle()
                V.tensor_tensor(yT[:, m, :], a, b, ALU.add).then_inc(s_yv, 1)
            n = 0
            for c in range(2):
                for t in range(NT):
                    n += 1
                    v.wait_ge(s_wo, n)
                    a = acc[:, t, c * 512:(c + 1) * 512]
                    V.tensor_tensor(a, a, pb[2 + 2 * c + t][:, :], ALU.add).then_inc(s_wov, 1)
            v.wait_ge(s_r3, 1)
            step(V.reciprocal(st[:, 14:16], st[:, 14:16]))
            settle()
            v.wait_ge(s_wov, 4)
            for t in range(NT):
                V.tensor_scalar(hN[:, t, :], acc[:, t, :], st[:, 14 + t:15 + t], None, ALU.mult).then_inc(s_r4, 1)
            for k in range(1, KT, 2):
                v.wait_ge(s_r5, k + 1)
                V.tensor_scalar(hn2T[:, k, :], pb[k][:, 0:TOK], cols[:, C_NFFN + k:C_NFFN + k + 1], None, ALU.mult).then_inc(s_hv, 1)
            for t in range(NT):
                v.wait_ge(s_lg, t + 1)
                step(V.tensor_tensor(lg[:, t, :], pb[t][:, 0:E], brt[:, :], ALU.add))
                settle()
                step(V.max(top[:, t, :], lg[:, t, :]))
                settle()
                V.tensor_scalar(st[:, 16 + t:17 + t], top[:, t, 0:1], -1.0, None, ALU.mult).then_inc(s_msk, 1)
            v.wait_ge(s_const, 7)
            for t in range(NT):
                step(V.max_index(topi[:, t, :], top[:, t, :], lg[:, t, :]))
            settle()
            for t in range(NT):
                step(V.tensor_copy(topf[:, t, :], topi[:, t, :]))
            settle()
            for t in range(NT):
                for k in range(TOPK):
                    idx = topf[:, t, k:k + 1]
                    if k == 0:
                        step(V.tensor_scalar(msk[:, t, :], iota[:, 0:E], idx, None, ALU.is_equal))
                    else:
                        settle()
                        ins = V.scalar_tensor_tensor(out=msk[:, t, :], in0=iota[:, 0:E], scalar=idx, in1=msk[:, t, :],
                                                     op0=ALU.is_equal, op1=ALU.add)
                        if k < TOPK - 1:
                            step(ins)
                        else:
                            ins.then_inc(s_msk, 1)
            v.wait_ge(s_msk, 4)
            v.wait_ge(s_ex, 2)
            for t in range(NT):
                step(V.tensor_tensor_reduce(out=gat[:, t, :], in0=gat[:, t, :], in1=msk[:, t, :], scale=1.0, scalar=0.0,
                                            op0=ALU.mult, op1=ALU.add, accum_out=st[:, 18 + t:19 + t]))
            settle()
            step(V.reciprocal(st[:, 18:20], st[:, 18:20]))
            settle()
            for t in range(NT):
                V.tensor_scalar(gat[:, t, :], gat[:, t, :], st[:, 18 + t:19 + t], None, ALU.mult).then_inc(s_gt, 1)
            v.wait_ge(s_gt, 2)
            for t in range(NT):
                step(V.tensor_copy(tab[:, :, 2 * FT + NT + t], gat[:, t, :]))
            v.wait_ge(s_pos, 2)
            for t in range(NT):
                step(V.scalar_tensor_tensor(out=lg2[:, t, :], in0=pb[2][:, t * E:(t + 1) * E], scalar=1.0, in1=msk[:, t, :], op0=ALU.add, op1=ALU.mult))
            settle()
            for t in range(NT):
                step(V.tensor_scalar(tab[:, :, 2 * FT + t], lg2[:, t, :], -1.0, None, ALU.add))
            settle()
            v.wait_ge(s_tab, 2)

            gain = cols[:, C_NFFN:C_NFFN + KT].unsqueeze(2).to_broadcast([P, KT, SLOTS])

            def stage(e, n, j):
                V.tensor_copy(tabE[:, j, :], tab[:, bass.ds(e, 1), :].rearrange("p a b -> p (a b)")).then_inc(m_te, 1)
                v.wait_ge(m_te, n + 1)

            def onehots(S, b, j):
                row = iota[:, b * SLOTS:(b + 1) * SLOTS]
                for t in range(NT):
                    slot = tabE[:, j, 2 * FT + t:2 * FT + t + 1]
                    gate = tabE[:, j, 2 * FT + NT + t:2 * FT + NT + t + 1]
                    V.tensor_scalar(oh[:, t, :], row, slot, None, ALU.is_equal).then_inc(S["oh"][0], 1)
                    V.tensor_scalar(og[:, t, :].rearrange("p (a s) -> p a s", a=2), row.unsqueeze(1).to_broadcast([P, 2, SLOTS]),
                                    slot, gate, ALU.is_equal, ALU.mult).then_inc(S["oh"][0], 1)

            def xg_copy(S, n, dst):
                wait(v, S, "ga", n)
                V.tensor_tensor(dst, pb[4].rearrange("p (k s) -> p k s", k=KT), gain, ALU.mult).then_inc(S["xg"][0], 1)

            def gu_copy(S, n):
                wait(v, S, "gu", n)
                V.tensor_copy(gu_s[:, 512:1024], pb[1]).then_inc(S["ev"][0], 1)

            def bias_clip(S, n, j):
                wait(v, S, "t", n)
                bias = tabE[:, j, 0:2 * FT].rearrange("p (f g) -> p f g", g=2)
                for b in range(2):
                    f = slice(b * FT // 2, (b + 1) * FT // 2)
                    V.tensor_tensor(tS[:, f, :, :], pb[2 + b].rearrange("p (f g s) -> p f g s", f=FT // 2, g=2),
                                    bias[:, f, :].unsqueeze(3).to_broadcast([P, FT // 2, 2, SLOTS]), ALU.add).then_inc(S["tb"][0], 1)
                wait(v, S, "tb", n, 2)
                V.tensor_scalar(tS[:, :, 0, :], tS[:, :, 0, :], 7.0, None, ALU.min).then_inc(S["g"][0], 1)
                V.tensor_scalar(tS[:, :, 1, :], tS[:, :, 1, :], 7.0, -7.0, ALU.min, ALU.max).then_inc(S["up"][0], 1)

            def swiglu(S, n):
                wait(v, S, "up", n)
                V.scalar_tensor_tensor(out=hid[:, :, :], in0=tS[:, :, 1, :], scalar=1.0, in1=tS[:, :, 0, :],
                                       op0=ALU.add, op1=ALU.mult).then_inc(S["a"][0], 1)
                wait(v, S, "a", n)
                wait(v, S, "sig", n)
                V.tensor_tensor(hid[:, :, :], hid[:, :, :], sg[:, :, :], ALU.mult).then_inc(S["hid"][0], 1)

            def add(S, n, t):
                wait(v, S, "sc", n, t + 1)
                a = acc[:, t, :].rearrange("p (c d) -> p c d", c=2)
                V.tensor_tensor(a, a, psum[:, 6:8, :], ALU.add).then_inc(S["add"][0], 1)

            def add_output_biases():
                for t in range(NT):
                    for c in range(2):
                        v.wait_ge(s_bm, 2 * t + c + 1)
                        a = acc[:, t, c * 512:(c + 1) * 512]
                        V.tensor_tensor(a, a, pb[6 + c], ALU.add).then_inc(s_bv, 1)
                v.wait_ge(s_bv, 4)

            def expert(e, j, first, last):
                if not last:
                    stage(e + 1, e + 1, 1 - j)
                    v.wait_ge(m_pt, e + 1)
                    onehots(MAIN, 0, 1 - j)
                gu_copy(MAIN, e)
                if first:
                    add_output_biases()
                else:
                    add(MAIN, e - 1, 0)
                bias_clip(MAIN, e, j)
                if not last:
                    xg_copy(MAIN, e + 1, xg)
                swiglu(MAIN, e)
                if not first:
                    add(MAIN, e - 1, 1)
                    v.wait_ge(m_add, 2 * e)
                more = v.value_load(ovi[0:1, 0, bass.ds(e, 1)], min_val=0, max_val=BLOCKS - 1)
                for b in range(1, BLOCKS):
                    with v.If(more > b - 1):
                        n = v.value_load(ovi[0:1, 1, bass.ds(e, 1)], min_val=0, max_val=E * BLOCKS) + (b - 1)
                        v.wait_ge(m_pt, e + (1 if last else 2))
                        wait(v, MAIN, "hid", e)
                        onehots(OVER, b, j)
                        xg_copy(OVER, n, xg_o)
                        gu_copy(OVER, n)
                        bias_clip(OVER, n, j)
                        swiglu(OVER, n)
                        for t in range(NT):
                            add(OVER, n, t)
                        wait(v, OVER, "add", n, 2)
                        v.sem_inc(s_over, 1)

            stage(0, 0, 0)
            onehots(MAIN, 0, 0)
            for b in range(1, BLOCKS):
                step(V.tensor_scalar(nov[:, b - 1, :], pb[3][0:E, 0:P], float(SLOTS * b), None, ALU.is_gt))
            settle()
            step(V.tensor_tensor(nov[:, 0, :], nov[:, 0, :], nov[:, 1, :], ALU.add))
            settle()
            V.tensor_tensor(nov[:, 2, :], nov[:, 0, :], nov[:, 2, :], ALU.add).then_inc(s_nov, 1)
            xg_copy(MAIN, 0, xg)
            v.wait_ge(s_ov, 1)
            V.tensor_copy(ovi[:, 0:2, :], pb[6][:, 0:2 * E].rearrange("p (a e) -> p a e", a=2)).then_inc(s_ovv, 1)
            V.tensor_scalar(ovi[:, 2, :], pb[6][:, 2 * E:3 * E], 1.0, 0.0, ALU.subtract, ALU.max).then_inc(s_ovv, 1)
            v.wait_ge(s_ovv, 2)
            for e in (0, 1):
                expert(e, e, e == 0, False)
            with v.Fori(1, E // 2 - 1) as i:
                for j in (0, 1):
                    expert(2 * i + j, j, False, False)
            for e in (E - 2, E - 1):
                expert(e, e % 2, False, e == E - 1)
            for t in range(NT):
                add(MAIN, E - 1, t)
            v.wait_ge(s_f3, 1)
            step(V.reciprocal(st[:, 22:24], st[:, 22:24]))
            settle()
            v.wait_ge(s_gf, 16)
            v.wait_ge(m_add, 2 * E)
            for t in range(NT):
                V.scalar_tensor_tensor(out=acc[:, t, :], in0=acc[:, t, :], scalar=st[:, 22 + t:23 + t], in1=gu_w[0][0][:, 0:D],
                                       op0=ALU.mult, op1=ALU.mult).then_inc(s_f4, 1)


_INS = ['x', 'meta_tokens', 'norm_mix_g', 'w_in', 'conv_qkv_w', 'a_log', 'dt_bias', 'dn_norm_g', 'w_dn_out',
        'b_glu', 'conv_dw_w', 'conv_dw_b', 'conv_ln_g', 'conv_ln_b', 'w_conv_out', 'b_conv_out', 'w_merge',
        'b_merge', 'w_out', 'norm_ffn_g', 'w_router', 'b_router', 'w_gate_up', 'b_gate_up', 'w_down', 'b_down',
        'final_norm_g']
_OUT = (1, 256, 1024)


def kernel(**inputs):
    import numpy as _np
    import concourse.bacc as _bacc
    from concourse import mybir as _mybir
    from concourse.bass_utils import run_bass_kernel_spmd as _run

    nc = _bacc.Bacc("TRN2", target_bir_lowering=False, num_devices=1)
    arrays, args = {}, []
    for name in _INS:
        a = _np.ascontiguousarray(inputs[name])
        arrays[f"in_{name}"] = a
        args.append(nc.dram_tensor(f"in_{name}", a.shape, _mybir.dt.from_np(a.dtype), kind="ExternalInput").ap())
    args.append(nc.dram_tensor("out_0", _OUT, _mybir.dt.float32, kind="ExternalOutput").ap())
    build(nc, *args)
    r = _run(nc, [arrays], core_ids=[0])
    return r.results[0]["out_0"]
```

```python
from contextlib import ExitStack

import numpy as np
import concourse.bass as bass
from concourse import mybir

F32 = mybir.dt.float32
I32 = mybir.dt.int32
ACT = mybir.ActivationFunctionType
ALU = mybir.AluOpType

P = 128
D = 1024
KT = D // P
TOK = 256
NT = TOK // P
META = 16
SEQ = META + TOK
H = 4
HW_ = H * P
TAPS = 4
CT = 4
WIDE = 31
PAD = WIDE - 1 - META
E = 32
TOPK = 4
FT = 8
SLOTS = 64
BLOCKS = TOK // SLOTS
EPS = 1e-6
LN_EPS = 1e-5
UNITS = [(META, 0), (P, META), (P, META + P)]

C_TAP = 0
C_BGLU = C_TAP + TAPS * 3 * H
C_DWB = C_BGLU + 2 * CT
C_LNG = C_DWB + CT
C_LNB = C_LNG + CT
C_BCONV = C_LNB + CT
C_BMERGE = C_BCONV + KT
C_NMIX = C_BMERGE + 2 * KT
C_NFFN = C_NMIX + KT
C_DN = C_NFFN + KT
N_COLS = C_DN + 1

Q0, K0, V0 = 0, 4, 8
GB0, GA0, GO0, MG0 = 12, 16, 20, 24
N_PROJ = 40
PROJ_BANKS = 3
TABW = 2 * FT + 2 * NT


def build(nc, x, meta_tokens, norm_mix_g, w_in, conv_qkv_w, a_log, dt_bias, dn_norm_g, w_dn_out,
          b_glu, conv_dw_w, conv_dw_b, conv_ln_g, conv_ln_b, w_conv_out, b_conv_out, w_merge,
          b_merge, w_out, norm_ffn_g, w_router, b_router, w_gate_up, b_gate_up, w_down, b_down,
          final_norm_g, out):
    with ExitStack() as ctx:
        def sb(name, shape, dt=F32):
            return ctx.enter_context(nc.sbuf_tensor(name, shape, dt))

        def sem(name):
            return ctx.enter_context(nc.semaphore(name))

        GU = 2 * FT * P
        ring = sb("ring", [P, 2 * KT * GU + FT * D])
        DN0 = 2 * KT * GU
        gu_w = [[ring[:, (s * KT + k) * GU:(s * KT + k + 1) * GU] for k in range(KT)] for s in range(2)]
        dn_w = [ring[:, DN0 + k * D:DN0 + (k + 1) * D] for k in range(FT)]
        mix_w = [ring[:, DN0 + s * 4 * D:DN0 + (s + 1) * 4 * D] for s in range(2)]

        def carve(base, limit):
            at = [base]

            def take(*shape):
                n = int(np.prod(shape))
                v = area[:, at[0]:at[0] + n]
                at[0] += n
                assert at[0] <= limit
                if len(shape) == 2:
                    return v.rearrange("p (a b) -> p a b", a=shape[0])
                if len(shape) == 3:
                    return v.rearrange("p (a b c) -> p a b c", a=shape[0], b=shape[1])
                return v
            return take

        area = ring
        setA = carve(0, KT * GU)
        qkv = setA(3 * H, SEQ)
        tmpA = setA(H, SEQ)
        tmpB = setA(H, SEQ)
        kbT = setA(H, SEQ)
        growE = setA(H, SEQ)
        gam = setA(3, H, P)
        qkT = setA(2, H, P)
        kB = setA(3, H, P)
        kD = setA(3, H, P)
        vB = setA(3, H, P)
        qdec = setA(2, H, P)
        flatA = ring[:, 3 * H * SEQ:3 * H * SEQ + 2 * H * SEQ]
        nwT = flatA[:, 0:2 * HW_].rearrange("p (u h c) -> p u h c", u=2, h=H)
        vn = flatA[:, 2 * HW_:3 * HW_].rearrange("p (h c) -> p h c", h=H)
        state = flatA[:, 3 * HW_:4 * HW_].rearrange("p (h c) -> p h c", h=H)

        setB = carve(KT * GU, 2 * KT * GU)
        gates = setB(2 * KT, TOK)
        hnT = setB(KT, SEQ)
        sgo = setB(H, TOK)
        uT = setB(CT, PAD + SEQ)
        ucT = setB(CT, TOK)
        oT = setB(H, TOK)
        yT = setB(KT, TOK)
        hn2T = setB(KT, TOK)
        wab = setB(KT, 2 * H)
        wr = setB(KT, E)
        xn = gates[:, 0:8, :].rearrange("p a b -> p (a b)").rearrange("p (t d) -> p t d", t=NT)
        xmn = gates[:, 8:12, :].rearrange("p a b -> p (a b)")
        xm = gates[:, 12:16, :].rearrange("p a b -> p (a b)")
        bgu_rows = yT[:, :, :].rearrange("p a b -> p (a b)")
        rowsA = hn2T[:, 0, 0:P]
        rowsB = hn2T[:, 1, 0:P]
        scr1 = yT[:, 0:4, :]
        scr2 = yT[:, 4:8, :]
        scr3 = hn2T[:, 0:4, :]

        work = sb("work", [P, 7808])
        area = work
        mixW = carve(0, 7808)
        lvl = mixW(7, P)
        aT = mixW(3, H, P)
        inv = mixW(3, H, P)
        invT = mixW(3, H, P)
        xlv = mixW(3, H, P)
        gbc = xlv
        bbc = invT
        t1 = aT[:, 0, :, :].rearrange("p a b -> p (a b)")
        moeW = carve(0, 7808)
        hN = moeW(NT, D)
        gu_s = moeW(2 * FT * SLOTS)
        tS = moeW(FT, 2, SLOTS)
        sg = moeW(FT, SLOTS)
        hid = moeW(FT, SLOTS)
        xg = moeW(KT, SLOTS)
        y_s = moeW(512)
        moeW(D - 512)
        og = moeW(NT, P)
        pT = moeW(2, TOK)
        oh = moeW(NT, SLOTS)
        gT = moeW(TOK)[0:E]
        hid_end = NT * D + 2 * FT * SLOTS + 2 * FT * SLOTS + 3 * FT * SLOTS
        bd = work[:, hid_end:hid_end + D]
        nov = sg[:, :, :].rearrange("p a b -> p (a b)")[0:E, 0:3 * P].rearrange("p (a c) -> p a c", a=3)
        tS_flat = tS[:, :, :, :].rearrange("p a b c -> p (a b c)")
        xg_o = tS_flat[:, 0:512].rearrange("p (k s) -> p k s", k=KT)
        y_o = gu_s[:, 0:512]
        pT_o = gu_s[:, 512:512 + TOK]
        acc = sb("acc", [P, NT, D])
        ident = sb("ident", [P, P])
        ones = sb("ones", [P, P])
        tri = sb("tri", [P, P])
        tris = sb("tris", [P, P])
        iota = sb("iota", [P, TOK])
        cols = sb("cols", [P, N_COLS])
        dwc = sb("dwc", [P, WIDE * CT])
        tab = sb("tab", [P, E, TABW])
        tabE = sb("tabE", [P, 2, TABW])
        ovi = sb("ovi", [P, 3, E], I32)
        ab = sb("ab", [P, 3, 2 * H])
        tok_s = sb("tok_s", [P, 12, 3, H])
        alog = sb("alog", [P, H])
        dtb = sb("dtb", [P, H])
        brt = sb("brt", [P, E])
        lg = sb("lg", [P, NT, E])
        lg2 = sb("lg2", [P, NT, E])
        msk = sb("msk", [P, NT, E])
        gat = sb("gat", [P, NT, E])
        top = sb("top", [P, NT, 8])
        topi = sb("topi", [P, NT, 8], mybir.dt.uint32)
        topf = sb("topf", [P, NT, 8])
        st = sb("st", [P, 32])
        eps = sb("eps", [P, 2])

        psum = ctx.enter_context(nc.psum_tensor("psum", [P, 8, 512], F32))
        pb = [psum[:, i, :] for i in range(8)]

        def heads(b, n=P, parts=P):
            return pb[b][0:parts, 0:H * n].rearrange("p (h c) -> p h c", h=H)

        s_x, s_meta, s_rows, s_small, s_bd = sem("x_in"), sem("meta_in"), sem("rows_in"), sem("small_in"), sem("bd_in")
        s_bgu, s_wab, s_wr, s_gf = sem("bgu_in"), sem("wab_in"), sem("wr_in"), sem("gf_in")
        s_mixw = [sem("mixw_in0"), sem("mixw_in1"), sem("mixw_in2")]
        s_gu = [[sem(f"gu_in{s}_{q}") for q in range(KT // 2)] for s in range(2)]
        s_dn = [sem(f"dn_in{k}") for k in range(4)]
        s_out = sem("out_stored")
        s_pool, s_const = sem("pool_step"), sem("consts_made")
        dve = sem("dve_step")
        s_ptr, s_cols, s_bgutr, s_tab = sem("params_turned"), sem("cols_ready"), sem("bgu_turned"), sem("tab_bias")
        s_ss, s_rt, s_xn = sem("x_squares"), sem("x_root"), sem("x_normed")
        s_ht, s_ha, s_hv = sem("h_turned"), sem("hnT_by_act"), sem("hnT_by_dve")
        s_proj, s_conv, s_gb, s_ga = sem("proj_done"), sem("conv_done"), sem("glu_gate"), sem("glu_out")
        s_gosig, s_go, s_gate = sem("go_sig"), sem("go_out"), sem("merge_gate")
        s_sgq, s_silu, s_sqq = sem("qkv_sig"), sem("qkv_silu"), sem("qk_squares")
        s_l2, s_l2r, s_qkn = sem("l2_sums"), sem("l2_roots"), sem("qk_normed")
        s_abm, s_abv, s_aba = sem("ab_done"), sem("ab_dve"), sem("ab_act")
        s_gbc, s_gr, s_brow, s_bbc = sem("g_bcast"), sem("gcum_rows"), sem("beta_rows"), sem("beta_bcast")
        s_gamx, s_game, s_gamm, s_gre = sem("gamma_diff"), sem("gamma_exp"), sem("gamma_masked"), sem("row_exp")
        s_sm, s_sme, s_smb, s_kb = sem("small_diffs"), sem("small_exps"), sem("small_beta"), sem("kb_ready")
        s_kt, s_ktv, s_kta = sem("kv_turned"), sem("kB_ready"), sem("kDvB_ready")
        s_at, s_atv, s_qd = sem("kk_done"), sem("at_ready"), sem("qdec_ready")
        s_lx, s_lxv, s_ly, s_lyv = sem("lvl_x"), sem("lvl_x_read"), sem("lvl_y"), sem("lvl_y_read")
        s_w, s_wa, s_v0, s_v0a, s_s0, s_s0a = sem("w_done"), sem("nw_ready"), sem("v0"), sem("v0_ready"), sem("s0"), sem("s0_ready")
        s_vn, s_vna, s_o, s_oa, s_su, s_sv = sem("vn"), sem("vn_ready"), sem("o"), sem("oT_ready"), sem("s_upd"), sem("state_ready")
        s_osq, s_on, s_onr, s_og = sem("o_squares"), sem("o_sums"), sem("o_roots"), sem("o_gated")
        s_uc, s_lm, s_lc, s_lsq, s_lv, s_lr = sem("wide_conv"), sem("ln_mean"), sem("ln_centred"), sem("ln_squares"), sem("ln_var"), sem("ln_root")
        s_ln, s_lnz, s_lnsig, s_u2 = sem("ln_scaled"), sem("ln_affine"), sem("ln_sig"), sem("u_ready")
        s_cb, s_cm, s_ab2, s_yv, s_wo, s_wov = sem("conv_branch"), sem("conv_gated"), sem("dn_branch"), sem("y_ready"), sem("out_done"), sem("h_ready")
        s_r1, s_r2, s_r3, s_r4, s_r5, s_r6 = sem("r_squares"), sem("r_meansq"), sem("r_root"), sem("r_normed"), sem("r_turned"), sem("hn2T_ready")
        s_lg, s_msk, s_ex, s_gt = sem("logits"), sem("masks_ready"), sem("r_exp"), sem("r_gates")
        s_pos, s_nov, s_ov, s_ovv, s_gtt, s_gtv, s_bm, s_bv = (sem("pos_done"), sem("nov_ready"), sem("ov_done"), sem("tables_ready"),
                                                               sem("gates_turned"), sem("gT_ready"), sem("bias_done"), sem("acc_ready"))
        m_oh, m_ga, m_pt, m_xg, m_ptc = sem("m_onehot"), sem("m_gathered"), sem("m_pt"), sem("m_xg"), sem("m_pt_copied")
        m_gu, m_ea, m_ev, m_t, m_g, m_sig, m_hid = sem("m_gu"), sem("m_gu_act"), sem("m_gu_dve"), sem("m_turned"), sem("m_gate"), sem("m_sig"), sem("m_hidden")
        m_y, m_ye, m_sc, m_add = sem("m_y"), sem("m_y_copied"), sem("m_scattered"), sem("m_added")
        o_pe, o_dve, o_act = sem("further_by_pe"), sem("further_by_dve"), sem("further_by_act")
        s_over = sem("further_blocks_over")
        m_te, m_tb, m_up, m_a = sem("m_staged"), sem("m_biased"), sem("m_up"), sem("m_product")
        s_f1, s_f3, s_f4 = sem("f_squares"), sem("f_root"), sem("f_out")

        MAIN = dict(oh=(m_oh, 4, 0), ga=(m_ga, 1, 0), pt=(m_pt, 1, 0), xg=(m_xg, 1, 0), ptc=(m_ptc, 1, 0), gu=(m_gu, KT // 2, KT // 2 - 1),
                    ea=(m_ea, 1, 0), ev=(m_ev, 1, 0), t=(m_t, 1, 0), tb=(m_tb, 2, 0), g=(m_g, 1, 0), up=(m_up, 1, 0),
                    a=(m_a, 1, 0), sig=(m_sig, 1, 0), hid=(m_hid, 1, 0), y=(m_y, FT // 2, FT // 2 - 1), ye=(m_ye, 1, 0), sc=(m_sc, 2, 0),
                    add=(m_add, 2, 0))
        PE_N, DVE_N, ACT_N = 5 + KT // 2 + FT // 2, 14, 4
        OVER = dict(ga=(o_pe, PE_N, 0), gu=(o_pe, PE_N, KT // 2), t=(o_pe, PE_N, KT // 2 + 1), pt=(o_pe, PE_N, KT // 2 + 2),
                    y=(o_pe, PE_N, KT // 2 + FT // 2 + 2), sc=(o_pe, PE_N, KT // 2 + FT // 2 + 3),
                    oh=(o_dve, DVE_N, 0), xg=(o_dve, DVE_N, 4), ev=(o_dve, DVE_N, 5), tb=(o_dve, DVE_N, 6),
                    g=(o_dve, DVE_N, 8), up=(o_dve, DVE_N, 9), a=(o_dve, DVE_N, 10), hid=(o_dve, DVE_N, 11),
                    add=(o_dve, DVE_N, 12), ea=(o_act, ACT_N, 0), ptc=(o_act, ACT_N, 1), sig=(o_act, ACT_N, 2), ye=(o_act, ACT_N, 3))

        def wait(eng, S, step, n, times=1):
            s, by_block, before = S[step]
            eng.wait_ge(s, n * by_block + (before + times))

        N_LVL = 7
        lvl_units = [[u for u in range(3) if (1 << l) < UNITS[u][0]] for l in range(N_LVL)]
        XB = {1: 3, 2: 5, 0: 7}
        YB = {1: 4, 2: 6, 0: 7}

        def turned(t, k):
            return pb[6 * t + k // 4][:, (k % 4) * P:(k % 4 + 1) * P]

        def l2_root(i):
            return growE[:, i, :] if i < H else tmpB[:, i - H, :]

        def beta_rows(u):
            if u == 0:
                return pb[3][:, H * META:2 * H * META].rearrange("p (h c) -> p h c", h=H)
            return heads(5 + u)

        def small_at(u, what):
            n, _ = UNITS[u]
            b = {"x": XB, "y": YB, "yt": XB}[what][u]
            o = {"x": 0, "y": 64, "yt": 128}[what] if u == 0 else 0
            return pb[b][0:n, o:o + H * n].rearrange("p (h c) -> p h c", h=H)

        def half(m, l, second):
            if len(m.shape) == 2:
                return m.rearrange("p (b t r) -> p b t r", t=2, r=1 << l)[:, :, second, :]
            return m.rearrange("p h (b t r) -> p h b t r", t=2, r=1 << l)[:, :, :, second, :]

        def packed(m, l, n):
            return m[:, :, 0:n // 2].rearrange("p h (b r) -> p h b r", r=1 << l)

        def mix_group(g):
            s = mix_w[g % 2] if g != 12 else ring[:, KT * GU + 2 * KT * TOK:KT * GU + 2 * KT * TOK + KT * 512]
            if g < 6:
                c0 = [0, HW_, 2 * HW_, 3 * HW_ + 2 * H + HW_ + 512, 3 * HW_ + 2 * H + HW_, 3 * HW_ + 2 * H][g]
                src = w_in[0][:, c0:c0 + 512].rearrange("(k p) n -> p k n", p=P)
            elif g < 10:
                src = w_merge[0][:, (g - 6) * 512:(g - 5) * 512].rearrange("(k p) n -> p k n", p=P)
            elif g < 12:
                src = (w_conv_out if g == 10 else w_dn_out)[0].rearrange("(k p) n -> p k n", p=P)
                return src, s.rearrange("p (k n) -> p k n", k=4)
            else:
                src = w_out[0][:, (g - 12) * 512:(g - 11) * 512].rearrange("(k p) n -> p k n", p=P)
            if g == 13:
                s = mix_w[0]
            return src, s.rearrange("p (k n) -> p k n", k=KT)

        def wait_mixw(eng, g):
            if g == 13:
                eng.wait_ge(s_mixw[2], 16)
                return
            eng.wait_ge(s_mixw[g % 2], 16 * (g // 2 + 1))

        ROWS = ((C_BGLU, C_DWB, b_glu), (C_DWB, C_LNG, conv_dw_b), (C_LNG, C_LNB, conv_ln_g), (C_LNB, C_BCONV, conv_ln_b),
                (C_BCONV, C_BMERGE, b_conv_out), (C_BMERGE, C_NMIX, b_merge), (C_NMIX, C_NFFN, norm_mix_g),
                (C_NFFN, C_DN, norm_ffn_g), (C_DN, N_COLS, dn_norm_g))

        def rows(eng, dst, src):
            eng.dma_start(dst, src).then_inc(s_rows, 16)

        block = ctx.enter_context(nc.Block())

        @block.sync
        def _(sp):
            def load_gate_up(e, s, q):
                dst = ring[:, (s * KT + 2 * q) * GU:(s * KT + 2 * q + 2) * GU].rearrange("p (k n) -> p k n", k=2)
                src = w_gate_up[0][e].rearrange("(q k p) n -> q p k n", p=P, k=2)[q]
                sp.dma_start(dst, src).then_inc(s_gu[s][q], 16)

            def load_down(e, q):
                dst = ring[:, DN0 + 2 * q * D:DN0 + 2 * (q + 1) * D].rearrange("p (k n) -> p k n", k=2)
                src = w_down[0][e].rearrange("(q k p) n -> q p k n", p=P, k=2)[q]
                sp.dma_start(dst, src).then_inc(s_dn[q], 16)

            sp.dma_start(acc[:, :, :], x[0].rearrange("(t p) d -> p t d", p=P)).then_inc(s_x, 16)
            for c0, c1, src in ROWS[4:]:
                rows(sp, rowsA[c0:c1, :], src[0].rearrange("(t c) -> t c", c=P))
            rows(sp, rowsB[0:WIDE * CT, :], conv_dw_w[0].rearrange("j (t c) -> (j t) c", c=P))
            for g in range(2):
                src, dst = mix_group(g)
                sp.dma_start(dst, src).then_inc(s_mixw[g % 2], 16)
            sp.dma_start(bgu_rows[0:E, :], b_gate_up[0]).then_inc(s_bgu, 16)
            sp.dma_start(wab, w_in[0][:, 3 * HW_:3 * HW_ + 2 * H].rearrange("(k p) n -> p k n", p=P)).then_inc(s_wab, 16)
            sp.dma_start(alog[:, :], a_log.to_broadcast([P, H])).then_inc(s_small, 16)
            sp.dma_start(dtb[:, :], dt_bias.to_broadcast([P, H])).then_inc(s_small, 16)
            sp.dma_start(brt[:, :], b_router.to_broadcast([P, E])).then_inc(s_small, 16)
            sp.dma_start(wr, w_router[0].rearrange("(k p) n -> p k n", p=P)).then_inc(s_wr, 16)
            for g in range(2, 12):
                sp.wait_ge(s_proj, 4 * (g - 1))
                src, dst = mix_group(g)
                sp.dma_start(dst, src).then_inc(s_mixw[g % 2], 16)
            sp.wait_ge(s_oa, 2)
            sp.dma_start(bd[0:E, :], b_down[0]).then_inc(s_bd, 16)
            for q in (0, 1):
                load_gate_up(0, 0, q)
            sp.wait_ge(s_og, 2)
            sp.dma_start(mix_group(12)[1], mix_group(12)[0]).then_inc(s_mixw[0], 16)
            sp.wait_ge(s_cb, KT)
            sp.dma_start(mix_group(13)[1], mix_group(13)[0]).then_inc(s_mixw[2], 16)
            for q in (2, 3):
                load_gate_up(0, 0, q)
            sp.wait_ge(s_yv, KT)
            load_gate_up(1, 1, 0)
            sp.wait_ge(s_wo, 3)
            load_gate_up(1, 1, 1)
            sp.wait_ge(s_wo, 4)
            load_gate_up(1, 1, 2)
            for q in range(FT // 2):
                load_down(0, q)
            sp.wait_ge(s_lg, NT)
            load_gate_up(1, 1, 3)

            def load_next(e, s, gate_up=True):
                if gate_up:
                    sp.wait_ge(m_gu, (KT // 2) * e + 1)
                    sp.sem_inc(s_over, 1)
                more = sp.value_load(ovi[0:1, 0, bass.ds(e, 1)], min_val=0, max_val=BLOCKS - 1)
                last = sp.value_load(ovi[0:1, 2, bass.ds(e, 1)], min_val=0, max_val=E * BLOCKS)
                with sp.If(more > 0):
                    for q in range(KT // 2 if gate_up else 0):
                        sp.wait_ge(o_pe, last * PE_N + (1 + q + 1))
                        sp.sem_inc(s_over, 1)
                        load_gate_up(e + 2, s, q)
                    for q in range(FT // 2):
                        sp.wait_ge(o_pe, last * PE_N + (1 + KT // 2 + 2 + q + 1))
                        sp.sem_inc(s_over, 1)
                        load_down(e + 1, q)
                with sp.If(more < 1):
                    for q in range(KT // 2 if gate_up else 0):
                        sp.wait_ge(m_gu, (KT // 2) * e + (q + 1))
                        sp.sem_inc(s_over, 1)
                        load_gate_up(e + 2, s, q)
                    for q in range(FT // 2):
                        sp.wait_ge(m_y, (FT // 2) * e + (q + 1))
                        sp.sem_inc(s_over, 1)
                        load_down(e + 1, q)

            sp.wait_ge(s_ovv, 2)
            with sp.Fori(0, E // 2 - 1) as i:
                for s in range(2):
                    load_next(2 * i + s, s)
            load_next(E - 2, 0, False)
            sp.dma_start(gu_w[0][0][:, 0:D], final_norm_g.rearrange("(a d) -> a d", a=1).to_broadcast([P, D])).then_inc(s_gf, 16)
            for t in range(NT):
                sp.wait_ge(s_f4, t + 1)
                sp.dma_start(out[0][t * P:(t + 1) * P, :], acc[:, t, :]).then_inc(s_out, 16)
            sp.wait_ge(s_out, 16 * NT)

        @block.gpsimd
        def _(pool):
            steps = [0]

            def link(ins):
                steps[0] += 1
                ins.then_inc(s_pool, 1)
                pool.wait_ge(s_pool, steps[0])

            pool.memset(ones[:, :], 1.0).then_inc(s_const, 1)
            pool.memset(eps[:, 0:1], EPS).then_inc(s_const, 1)
            pool.memset(eps[:, 1:2], LN_EPS).then_inc(s_const, 1)
            pool.wait_ge(s_const, 3)
            link(pool.memset(ident[:, :], 0.0))
            pool.affine_select(out=ident[:, :], in_=ident[:, :], compare_op=ALU.not_equal, fill=1.0, base=0,
                               pattern=[[-1, P]], channel_multiplier=1).then_inc(s_const, 1)
            pool.affine_select(out=tri[:, :], in_=ones[:, :], compare_op=ALU.is_ge, fill=0.0, base=0,
                               pattern=[[1, P]], channel_multiplier=-1).then_inc(s_const, 1)
            pool.affine_select(out=tris[:, :], in_=ones[:, :], compare_op=ALU.is_gt, fill=0.0, base=0,
                               pattern=[[1, P]], channel_multiplier=-1).then_inc(s_const, 1)
            link(pool.memset(lvl[:, :, :], 0.0))
            for l in range(N_LVL):
                s = 1 << l
                nb = P // (2 * s)
                v = lvl[:, l, :].rearrange("p (b h r) -> p b h r", h=2, r=s)[:, :, 0, :]
                src = ones[:, 0:P // 2].rearrange("p (b r) -> p b r", r=s)
                link(pool.affine_select(out=v, in_=src, compare_op=ALU.is_ge, fill=0.0, base=-s,
                                        pattern=[[-2 * s, nb], [0, s]], channel_multiplier=1))
                link(pool.affine_select(out=v, in_=v, compare_op=ALU.is_ge, fill=0.0, base=2 * s - 1,
                                        pattern=[[2 * s, nb], [0, s]], channel_multiplier=-1))
            pool.iota(iota[:, :], pattern=[[1, TOK]], base=0, channel_multiplier=0,
                      allow_small_or_imprecise_dtypes=True).then_inc(s_const, 1)

        @block.scalar
        def _(sc):
            sc.dma_start(xm[0:META, :], meta_tokens).then_inc(s_meta, 16)
            rows(sc, rowsA[C_TAP:C_BGLU, :], conv_qkv_w[0].rearrange("j (t c) -> (j t) c", c=P))
            for c0, c1, src in ROWS[:4]:
                rows(sc, rowsA[c0:c1, :], src[0].rearrange("(t c) -> t c", c=P))

            sc.wait_ge(s_const, 3)
            nc.scalar.activation(st[:, 30:31], eps[:, 0:1], ACT.Sqrt)
            sc.wait_ge(s_x, 16)
            for t in range(NT):
                nc.scalar.activation(xn[:, t, :], acc[:, t, :], ACT.Square, accum_out=st[:, t:t + 1]).then_inc(s_ss, 1)
            sc.wait_ge(s_meta, 16)
            nc.scalar.activation(xmn[0:META, :], xm[0:META, :], ACT.Square, accum_out=st[0:META, 2:3]).then_inc(s_ss, 1)
            sc.wait_ge(s_ss, 3)
            nc.scalar.activation(st[:, 4:6], st[:, 0:2], ACT.Sqrt, bias=eps[:, 0:1], scale=1.0 / D).then_inc(s_rt, 1)
            nc.scalar.activation(st[0:META, 6:7], st[0:META, 2:3], ACT.Sqrt, bias=eps[0:META, 0:1], scale=1.0 / D).then_inc(s_rt, 1)
            sc.wait_ge(s_cols, 2)
            for k in range(0, KT, 2):
                sc.wait_ge(s_ht, k + 1)
                nc.scalar.activation(hnT[:, k, :], pb[k % 8][:, 0:SEQ], ACT.Copy, scale=cols[:, C_NMIX + k:C_NMIX + k + 1]).then_inc(s_ha, 1)
            for r in range(2):
                sc.wait_ge(s_conv, 4 * (r + 1))
                if r == 1:
                    sc.wait_ge(s_silu, r)
                nc.scalar.activation(tmpA, qkv[:, 4 * r:4 * r + 4, :], ACT.Sigmoid).then_inc(s_sgq, 1)
                sc.wait_ge(s_silu, r + 1)
                if r == 1:
                    sc.wait_ge(s_l2, H)
                nc.scalar.activation(tmpB, qkv[:, 4 * r:4 * r + 4, :], ACT.Square).then_inc(s_sqq, 1)
            for i in range(2 * H):
                sc.wait_ge(s_l2, i + 1)
                nc.scalar.activation(l2_root(i), pb[3 + i % 4][:, 0:SEQ], ACT.Sqrt, bias=eps[:, 0:1]).then_inc(s_l2r, 1)
            sc.wait_ge(s_conv, 12)
            nc.scalar.activation(tmpA, qkv[:, 8:12, :], ACT.Sigmoid).then_inc(s_sgq, 1)
            sc.wait_ge(s_abv, 2)
            nc.scalar.activation(tok_s[:, 2, :, :], tok_s[:, 1, :, :], ACT.Exp, scale=-1.0).then_inc(s_aba, 1)
            nc.scalar.activation(tok_s[:, 4, :, :], ab[:, :, H:2 * H], ACT.Exp, scale=-1.0).then_inc(s_aba, 1)
            sc.wait_ge(s_small, 48)
            nc.scalar.activation(st[:, 8:8 + H], alog[:, :], ACT.Exp).then_inc(s_aba, 1)
            sc.wait_ge(s_aba, 3)
            nc.scalar.activation(tok_s[:, 3, :, :], tok_s[:, 2, :, :], ACT.Ln, bias=ones[:, 0:1]).then_inc(s_aba, 1)
            for i in range(CT):
                sc.wait_ge(s_proj, GB0 + i + 1)
                sc.wait_ge(s_qkn, i + 1)
                nc.scalar.activation(growE[:, i, :], pb[(GB0 + i) % PROJ_BANKS][:, 0:SEQ], ACT.Sigmoid,
                                     bias=cols[:, C_BGLU + CT + i:C_BGLU + CT + i + 1]).then_inc(s_gb, 1)
            for u, (n, c0) in enumerate(UNITS):
                sc.wait_ge(s_gamx, H * (u + 1))
                v = gam[0:n, u, :, 0:n]
                nc.scalar.activation(v, v, ACT.Exp).then_inc(s_game, 1)
                if u == 0:
                    sc.wait_ge(s_ga, CT)
                    continue
                sc.wait_ge(s_sm, u + 1)
                nc.scalar.activation(growE[:, :, c0:c0 + n], heads(3 + u, n), ACT.Exp).then_inc(s_gre, 1)
            sc.wait_ge(s_sm, 3)
            nc.scalar.activation(tok_s[:, 8:10, :, :], tok_s[:, 6:8, :, :], ACT.Exp).then_inc(s_sme, 1)
            sc.wait_ge(s_sme, 1)
            sc.wait_ge(s_smb, 1)
            for u, (n, c0) in enumerate(UNITS):
                sc.wait_ge(s_kt, 2 * u + 2)
                sc.wait_ge(s_ktv, H * (u + 1))
                kb_, vb_ = (3, 4) if u % 2 == 0 else (5, 6)
                for h in range(H):
                    nc.scalar.activation(kD[0:n, u, h, :], heads(kb_, P, n)[:, h, :], ACT.Copy, scale=tok_s[0:n, 9, u, h:h + 1]).then_inc(s_kta, 1)
                    nc.scalar.activation(vB[0:n, u, h, :], heads(vb_, P, n)[:, h, :], ACT.Copy, scale=tok_s[0:n, 5, u, h:h + 1]).then_inc(s_kta, 1)
            for i in range(4):
                sc.wait_ge(s_proj, GO0 + i + 1)
                nc.scalar.activation(scr2[:, i, :], pb[(GO0 + i) % PROJ_BANKS][:, 0:TOK], ACT.Sigmoid).then_inc(s_gosig, 1)
            def merge_gate(i):
                sc.wait_ge(s_proj, MG0 + i + 1)
                nc.scalar.activation(gates[:, i, :], pb[(MG0 + i) % PROJ_BANKS][:, 0:TOK], ACT.Sigmoid,
                                     bias=cols[:, C_BMERGE + i:C_BMERGE + i + 1]).then_inc(s_gate, 1)

            for i in range(2 * KT - 5):
                merge_gate(i)
            for u in (1, 2):
                sc.wait_ge(s_w, u)
                nc.scalar.activation(nwT[:, u - 1, :, :], heads(2 + u), ACT.Copy, scale=-1.0).then_inc(s_wa, 1)
            sc.wait_ge(s_v0, 1)
            nc.scalar.activation(vn[0:META, :, :], heads(5, P, META), ACT.Copy).then_inc(s_v0a, 1)
            merge_gate(2 * KT - 5)
            sc.wait_ge(s_s0, 1)
            nc.scalar.activation(state[:, :, :], heads(6), ACT.Copy).then_inc(s_s0a, 1)
            sc.wait_ge(s_lc, CT)
            nc.scalar.activation(scr3, ucT, ACT.Square).then_inc(s_lsq, 1)
            merge_gate(2 * KT - 4)

            def new_values(u):
                sc.wait_ge(s_vn, u)
                nc.scalar.activation(vn[:, :, :], heads(7), ACT.Copy).then_inc(s_vna, 1)

            def output(u):
                c = slice((u - 1) * P, u * P)
                sc.wait_ge(s_o, u)
                nc.scalar.activation(oT[:, :, c], heads(3), ACT.Copy).then_inc(s_oa, 1)
                sc.wait_ge(s_oa, u)
                if u == 1:
                    sc.wait_ge(s_go, 4)
                nc.scalar.activation(scr1[:, :, c], oT[:, :, c], ACT.Square).then_inc(s_osq, 1)

            new_values(1)
            sc.wait_ge(s_lv, 1)
            nc.scalar.activation(t1[:, 0:TOK], pb[6][:, 0:TOK], ACT.Sqrt, bias=eps[:, 1:2], scale=1.0 / (CT * P)).then_inc(s_lr, 1)
            merge_gate(2 * KT - 3)
            output(1)
            sc.wait_ge(s_lnz, CT)
            nc.scalar.activation(scr3, ucT, ACT.Sigmoid).then_inc(s_lnsig, 1)
            merge_gate(2 * KT - 2)
            new_values(2)
            merge_gate(2 * KT - 1)
            output(2)
            for u in (1, 2):
                sc.wait_ge(s_on, u)
                nc.scalar.activation(scr2[:, :, (u - 1) * P:u * P], heads(3 + u), ACT.Sqrt, bias=eps[:, 0:1], scale=1.0 / P).then_inc(s_onr, 1)
            def squares(t, c):
                n = NT * t + c
                sc.wait_ge(s_wov, n + 1)
                nc.scalar.activation(hN[:, t, c * 512:(c + 1) * 512], acc[:, t, c * 512:(c + 1) * 512], ACT.Square,
                                     accum_out=st[:, 24 + n:25 + n]).then_inc(s_r1, 1)

            def root(t):
                sc.wait_ge(s_r2, t + 1)
                nc.scalar.activation(st[:, 14 + t:15 + t], st[:, 12 + t:13 + t], ACT.Sqrt, bias=eps[:, 0:1], scale=1.0 / D).then_inc(s_r3, 1)

            def scaled(t):
                sc.wait_ge(s_r5, t + 1)
                for k in range(4, KT):
                    nc.scalar.activation(hn2T[:, k, t * P:(t + 1) * P], turned(t, k), ACT.Copy, scale=cols[:, C_NFFN + k:C_NFFN + k + 1]).then_inc(s_r6, 1)

            squares(0, 0)
            squares(0, 1)
            root(0)
            squares(1, 0)
            scaled(0)
            squares(1, 1)
            root(1)
            scaled(1)
            for t in range(NT):
                sc.wait_ge(s_msk, 2 * t + 1)
                nc.scalar.activation(gat[:, t, :], lg[:, t, :], ACT.Exp, bias=st[:, 16 + t:17 + t]).then_inc(s_ex, 1)

            def gu_copy(S, n):
                wait(sc, S, "gu", n)
                nc.scalar.activation(gu_s[:, 0:512], pb[0][:, :], ACT.Copy).then_inc(S["ea"][0], 1)

            def pt_copy(S, n, dst):
                wait(sc, S, "pt", n)
                nc.scalar.activation(dst, pb[5][:, 0:TOK], ACT.Copy).then_inc(S["ptc"][0], 1)

            def sigmoid(S, n):
                wait(sc, S, "g", n)
                nc.scalar.activation(sg[:, :, :], tS[:, :, 0, :], ACT.Sigmoid, scale=1.702).then_inc(S["sig"][0], 1)

            def y_copy(S, n, dst):
                wait(sc, S, "y", n)
                nc.scalar.activation(dst, pb[5][:, :], ACT.Copy).then_inc(S["ye"][0], 1)

            def expert(e, j, first, last):
                gu_copy(MAIN, e)
                sigmoid(MAIN, e)
                if not last:
                    pt_copy(MAIN, e + 1, pT[:, 1 - j, :])
                if first:
                    sc.wait_ge(s_bm, 4)
                else:
                    sc.wait_ge(m_sc, 2 * e)
                y_copy(MAIN, e, y_s)
                more = sc.value_load(ovi[0:1, 0, bass.ds(e, 1)], min_val=0, max_val=BLOCKS - 1)
                for b in range(1, BLOCKS):
                    with sc.If(more > b - 1):
                        n = sc.value_load(ovi[0:1, 1, bass.ds(e, 1)], min_val=0, max_val=E * BLOCKS) + (b - 1)
                        gu_copy(OVER, n)
                        pt_copy(OVER, n, pT_o)
                        sigmoid(OVER, n)
                        y_copy(OVER, n, y_o)

            pt_copy(MAIN, 0, pT[:, 0, :])
            sc.wait_ge(s_gtt, 1)
            nc.scalar.activation(gT[:, :], pb[2][0:E, 0:TOK], ACT.Copy).then_inc(s_gtv, 1)
            sc.wait_ge(s_ovv, 2)
            for e in (0, 1):
                expert(e, e, e == 0, False)
            with sc.Fori(1, E // 2 - 1) as i:
                for j in (0, 1):
                    expert(2 * i + j, j, False, False)
            for e in (E - 2, E - 1):
                expert(e, e % 2, False, e == E - 1)
            nc.scalar.activation(st[:, 31:32], eps[:, 0:1], ACT.Sqrt)
            for t in range(NT):
                sc.wait_ge(m_add, 2 * (E - 1) + 1 + t)
                nc.scalar.activation(hN[:, t, :], acc[:, t, :], ACT.Square, accum_out=st[:, 20 + t:21 + t]).then_inc(s_f1, 1)
                sc.wait_ge(s_f1, t + 1)
                nc.scalar.activation(st[:, 22 + t:23 + t], st[:, 20 + t:21 + t], ACT.Sqrt, bias=eps[:, 0:1], scale=1.0 / D).then_inc(s_f3, 1)

        @block.tensor
        def _(pe):
            def mm(o, l, r, a=True, z=True, **kw):
                return nc.tensor.matmul(o, l, r, start=a, stop=z, **kw)

            pe.wait_ge(s_const, 4)
            pe.wait_ge(s_rows, 16 * 11)
            nc.tensor.transpose(pb[0][:, 0:N_COLS], rowsA[0:N_COLS, :], ident[0:N_COLS, 0:N_COLS]).then_inc(s_ptr, 1)
            nc.tensor.transpose(pb[1][:, 0:WIDE * CT], rowsB[0:WIDE * CT, :], ident[0:WIDE * CT, 0:WIDE * CT]).then_inc(s_ptr, 1)
            pe.wait_ge(s_cols, 2)
            for k in range(KT):
                if k == 0:
                    pe.wait_ge(s_xn, 3)
                for n, c0 in UNITS:
                    src = xmn[0:META, k * P:(k + 1) * P] if n == META else xn[:, (c0 - META) // P, k * P:(k + 1) * P]
                    last = nc.tensor.transpose(pb[k][:, c0:c0 + n], src, ident[0:n, 0:n])
                last.then_inc(s_ht, 1)
            pe.wait_ge(s_ha, KT // 2)
            pe.wait_ge(s_hv, KT // 2)

            def freed(i):
                for first, s in ((MG0, s_gate), (GO0, s_go), (GA0, s_ga), (GB0, s_gb), (0, s_conv)):
                    if i >= first:
                        pe.wait_ge(s, i - first + 1)
                        return

            def project(i):
                if i >= PROJ_BANKS:
                    freed(i - PROJ_BANKS)
                g = i // 4
                wait_mixw(pe, g)
                _, w = mix_group(g)
                c0 = META if i >= GO0 else 0
                for k in range(KT):
                    last = mm(pb[i % PROJ_BANKS][:, 0:SEQ - c0], w[:, k, (i % 4) * P:(i % 4 + 1) * P], hnT[:, k, c0:SEQ],
                              k == 0, k == KT - 1)
                last.then_inc(s_proj, 1)

            def l2_sum(i):
                if i >= 4:
                    pe.wait_ge(s_l2r, i - 3)
                mm(pb[3 + i % 4][:, 0:SEQ], ones[:, :], tmpB[:, i % H, :]).then_inc(s_l2, 1)

            for i in range(K0):
                project(i)
            pe.wait_ge(s_bgu, 16)
            for f in range(2 * FT):
                last = nc.tensor.transpose(pb[7][:, f * E:(f + 1) * E], bgu_rows[0:E, f * P:(f + 1) * P], ident[0:E, 0:E])
            last.then_inc(s_bgutr, 1)
            for i in range(K0, V0):
                project(i)
            pe.wait_ge(s_sqq, 1)
            for i in range(H):
                l2_sum(i)
            for i in range(V0, GB0):
                project(i)
                if i == GB0 - 2:
                    pe.wait_ge(s_sqq, 2)
                    for h in range(H, 2 * H):
                        l2_sum(h)
            pe.wait_ge(s_wab, 16)
            pe.wait_ge(s_tab, 2)
            for u, (n, c0) in enumerate(UNITS):
                for k in range(KT):
                    last = mm(pb[7][0:n, 2 * H * u:2 * H * (u + 1)], hnT[:, k, c0:c0 + n], wab[:, k, :], k == 0, k == KT - 1)
                last.then_inc(s_abm, 1)
            for i in range(GB0, GO0):
                project(i)
            pe.wait_ge(s_const, 6)
            pe.wait_ge(s_l2r, 2 * H)
            for u, (n, c0) in enumerate(UNITS):
                pe.wait_ge(s_gbc, u + 1)
                for h in range(H):
                    last = mm(heads(3 + u, n)[:, h, :], gbc[0:n, u, h, :], tri[0:n, 0:n])
                last.then_inc(s_gr, 1)
            for u, (n, c0) in enumerate(UNITS):
                pe.wait_ge(s_bbc, u + 1)
                for h in range(H):
                    last = mm(beta_rows(u)[:, h, :], bbc[0:n, u, h, :], ident[0:n, 0:n])
                last.then_inc(s_brow, 1)
            project(GO0)
            pe.wait_ge(s_sm, 3)
            pe.wait_ge(s_gre, 2)
            pe.wait_ge(s_kb, 3)
            for u, (n, c0) in enumerate(UNITS):
                kb_, vb_ = (3, 4) if u % 2 == 0 else (5, 6)
                if u == 2:
                    project(GO0 + 1)
                    pe.wait_ge(s_ktv, 4)
                    pe.wait_ge(s_kta, 8)
                for base, b in ((K0, kb_), (V0, vb_)):
                    for h in range(H):
                        last = nc.tensor.transpose(heads(b, P, n)[:, h, :], qkv[:, base + h, c0:c0 + n], ident[:, :])
                    last.then_inc(s_kt, 1)
            project(GO0 + 2)
            for u, (n, c0) in enumerate(UNITS):
                if u == 0:
                    pe.wait_ge(s_ktv, 12)
                    pe.wait_ge(s_kta, 24)
                for h in range(H):
                    last = mm(heads(3 + u, n, n)[:, h, :], qkv[:, K0 + h, c0:c0 + n], kbT[:, h, c0:c0 + n])
                last.then_inc(s_at, 1)
            for u in (1, 2):
                n, c0 = UNITS[u]
                for h in range(H):
                    last = mm(heads(5 + u)[:, h, :], qkv[:, K0 + h, c0:c0 + n], qkv[:, Q0 + h, c0:c0 + n])
                last.then_inc(s_at, 1)
            project(GO0 + 3)
            nxt = [MG0]

            def fill(count, until=N_PROJ - 5):
                for _ in range(count):
                    if nxt[0] < until:
                        project(nxt[0])
                        nxt[0] += 1

            pe.wait_ge(s_atv, 5)
            nx = 0
            solved = 3
            for l in range(N_LVL):
                pe.wait_ge(s_lyv, solved)
                for u in lvl_units[l]:
                    n, _ = UNITS[u]
                    for h in range(H):
                        last = mm(small_at(u, "x")[:, h, 0:n // 2], aT[0:n, u, h, 0:n], half(inv[0:n, u, h, 0:n], l, 0))
                    last.then_inc(s_lx, 1)
                fill(1)
                for u in lvl_units[l]:
                    n, _ = UNITS[u]
                    nx += 1
                    pe.wait_ge(s_lxv, nx)
                    if l > 0 and 4 << l <= n:
                        for h in range(H):
                            mm(small_at(u, "y")[:, h, 0:n // 2], invT[0:n, u, h, 0:n], half(xlv[0:n, u, h, 0:n], l, 0))
                    for h in range(H):
                        last = mm(small_at(u, "yt")[:, h, 0:n // 2], xlv[0:n, u, h, 0:n], half(invT[0:n, u, h, 0:n], l, 1))
                    last.then_inc(s_ly, 1)
                solved += len(lvl_units[l])
                if l % 2 == 0:
                    fill(1)
            fill(N_PROJ)
            pe.wait_ge(s_lyv, solved)
            for u in (1, 2):
                for h in range(H):
                    last = mm(heads(2 + u)[:, h, :], kB[:, u, h, :], invT[:, u, h, :])
                last.then_inc(s_w, 1)
            for h in range(H):
                last = mm(heads(5, P, META)[:, h, :], invT[0:META, 0, h, 0:META], vB[0:META, 0, h, :])
            last.then_inc(s_v0, 1)
            fill(1, N_PROJ)
            pe.wait_ge(s_v0a, 1)
            for h in range(H):
                last = mm(heads(6)[:, h, :], kD[0:META, 0, h, :], vn[0:META, h, :])
            last.then_inc(s_s0, 1)
            pe.wait_ge(s_uc, CT)
            for c in range(CT):
                last = mm(pb[5][:, 0:TOK], ones[:, :], ucT[:, c, :], c == 0, c == CT - 1)
            last.then_inc(s_lm, 1)
            fill(1, N_PROJ)

            def new_values(u):
                for h in range(H):
                    mm(heads(7)[:, h, :], invT[:, u, h, :], vB[:, u, h, :], True, False)
                    last = mm(heads(7)[:, h, :], nwT[:, u - 1, h, :], state[:, h, :], False, True)
                last.then_inc(s_vn, 1)

            def output(u):
                pe.wait_ge(s_vna, u)
                for h in range(H):
                    mm(heads(3)[:, h, :], state[:, h, :], qdec[:, u - 1, h, :], True, False)
                    last = mm(heads(3)[:, h, :], vn[:, h, :], qkT[:, u - 1, h, :], False, True)
                last.then_inc(s_o, 1)

            def head_squares(u):
                pe.wait_ge(s_osq, u)
                mm(heads(3 + u), ones[:, :], scr1[:, :, (u - 1) * P:u * P]).then_inc(s_on, 1)

            pe.wait_ge(s_qd, 2)
            pe.wait_ge(s_wa, 2)
            pe.wait_ge(s_s0a, 1)
            new_values(1)
            pe.wait_ge(s_lsq, 1)
            for c in range(CT):
                last = mm(pb[6][:, 0:TOK], ones[:, :], scr3[:, c, :], c == 0, c == CT - 1)
            last.then_inc(s_lv, 1)
            fill(1, N_PROJ)
            output(1)
            for h in range(H):
                last = mm(heads(4)[:, h, :], kD[:, 1, h, :], vn[:, h, :])
            last.then_inc(s_su, 1)
            fill(1, N_PROJ)
            pe.wait_ge(s_sv, H)
            new_values(2)
            head_squares(1)
            fill(1, N_PROJ)
            output(2)

            wait_mixw(pe, 10)
            _, wc = mix_group(10)
            pe.wait_ge(s_u2, 1)
            for m in range(KT):
                if m < PROJ_BANKS:
                    pe.wait_ge(s_gate, 2 * KT)
                else:
                    pe.wait_ge(s_cm, m - PROJ_BANKS + 1)
                for c in range(4):
                    last = mm(pb[m % PROJ_BANKS][:, 0:TOK], wc[:, c, m * P:(m + 1) * P], ucT[:, c, :], c == 0, c == 3)
                last.then_inc(s_cb, 1)
                if m == 1:
                    head_squares(2)
            wait_mixw(pe, 11)
            _, wd = mix_group(11)
            pe.wait_ge(s_og, 2)
            for m in range(KT):
                if m >= 2:
                    pe.wait_ge(s_yv, m - 1)
                for c in range(4):
                    last = mm(pb[6 + m % 2][:, 0:TOK], wd[:, c, m * P:(m + 1) * P], oT[:, c, :], c == 0, c == 3)
                last.then_inc(s_ab2, 1)
            def out_tile(t, c):
                wait_mixw(pe, 12 + c)
                _, w = mix_group(12 + c)
                for k in range(KT):
                    if c == 0 and t == 0:
                        pe.wait_ge(s_yv, k + 1)
                    last = mm(pb[2 + 2 * c + t][:, :], yT[:, k, t * P:(t + 1) * P], w[:, k, :], k == 0, k == KT - 1)
                last.then_inc(s_wo, 1)

            def turn_router(t):
                pe.wait_ge(s_r4, t + 1)
                for k in range(KT):
                    last = nc.tensor.transpose(turned(t, k), hN[:, t, k * P:(k + 1) * P], ident[:, :])
                last.then_inc(s_r5, 1)

            def logits(t):
                pe.wait_ge(s_wr, 16)
                pe.wait_ge(s_r6, 4 * (t + 1))
                pe.wait_ge(s_hv, KT // 2 + t + 1)
                for k in range(KT):
                    last = mm(pb[2 + 2 * t][:, 0:E], hn2T[:, k, t * P:(t + 1) * P], wr[:, k, :], k == 0, k == KT - 1)
                last.then_inc(s_lg, 1)

            out_tile(0, 0)
            out_tile(0, 1)
            out_tile(1, 0)
            turn_router(0)
            out_tile(1, 1)
            logits(0)
            turn_router(1)
            logits(1)
            pe.wait_ge(s_msk, 4)
            mm(pb[0][:, 0:E], tris[:, :], msk[:, 0, :])
            mm(pb[0][:, E:2 * E], tris[:, :], msk[:, 1, :], True, False)
            mm(pb[0][:, E:2 * E], ones[:, :], msk[:, 0, :], False, True).then_inc(s_pos, 1)
            for t in range(NT):
                last = mm(pb[3][0:E, 0:P], msk[:, t, :], ones[:, :], t == 0, t == NT - 1)
            last.then_inc(s_pos, 1)

            def gather(S, n):
                wait(pe, S, "oh", n, 2 * NT)
                for k in range(KT):
                    for t in range(NT):
                        last = mm(pb[4][:, k * SLOTS:(k + 1) * SLOTS], hN[:, t, k * P:(k + 1) * P], oh[:, t, :], t == 0, t == NT - 1)
                last.then_inc(S["ga"][0], 1)

            def turn_pt(S, n):
                for t in range(NT):
                    last = nc.tensor.transpose(pb[5][:, t * P:(t + 1) * P], og[:, t, :], ident[:, :])
                last.then_inc(S["pt"][0], 1)

            def gate_up(S, n, j, src, arrived):
                wait(pe, S, "xg", n)
                for k in range(KT):
                    if arrived is not None and k % 2 == 0:
                        pe.wait_ge(s_gu[j][k // 2], arrived)
                    for c in range(2):
                        mm(pb[c][0:SLOTS, :], src[:, k, :], gu_w[j][k][:, c * 512:(c + 1) * 512], k == 0, k == KT - 1)
                        last = mm(pb[c][SLOTS:P, :], src[:, k, :], gu_w[j][k][:, D + c * 512:D + (c + 1) * 512], k == 0, k == KT - 1)
                    if k % 2:
                        last.then_inc(S["gu"][0], 1)

            def turn_gu(S, n):
                wait(pe, S, "ea", n)
                wait(pe, S, "ev", n)
                for f in range(FT):
                    last = nc.tensor.transpose(pb[2 + f // 4][:, (f % 4) * P:(f % 4 + 1) * P], gu_s[:, f * P:(f + 1) * P], ident[:, :])
                last.then_inc(S["t"][0], 1)

            def down(S, n, arrived):
                wait(pe, S, "hid", n)
                for f in range(FT):
                    if arrived is not None and f % 2 == 0:
                        pe.wait_ge(s_dn[f // 2], arrived)
                    for c in range(2):
                        last = mm(pb[5][c * SLOTS:(c + 1) * SLOTS, :], hid[:, f, :], dn_w[f][:, c * 512:(c + 1) * 512], f == 0, f == FT - 1)
                    if f % 2:
                        last.then_inc(S["y"][0], 1)

            def scatter(S, n, t, w, y):
                for c in range(2):
                    r = slice(c * SLOTS, (c + 1) * SLOTS)
                    last = mm(pb[6 + c][:, :], w[r, t * P:(t + 1) * P], y[r, :])
                last.then_inc(S["sc"][0], 1)

            def output_biases():
                pe.wait_ge(s_ovv, 2)
                pe.wait_ge(s_bd, 16)
                for t in range(NT):
                    for c in range(2):
                        if t == 1:
                            pe.wait_ge(s_bv, c + 1)
                        mm(pb[6 + c][:, :], gT[:, t * P:(t + 1) * P], bd[0:E, c * 512:(c + 1) * 512]).then_inc(s_bm, 1)

            def expert(e, i, j, first, second, last_e):
                gate_up(MAIN, e, j, xg, 16 * (i + 1))
                if not first:
                    pe.wait_ge(m_ye, e)
                    if second:
                        pe.wait_ge(s_bv, 4)
                    else:
                        pe.wait_ge(m_add, 2 * e - 2)
                    scatter(MAIN, e - 1, 0, pT[:, 1 - j, :], y_s)
                turn_gu(MAIN, e)
                if not last_e:
                    gather(MAIN, e + 1)
                if not first:
                    pe.wait_ge(m_add, 2 * e - 1)
                    scatter(MAIN, e - 1, 1, pT[:, 1 - j, :], y_s)
                if not last_e:
                    turn_pt(MAIN, e + 1)
                    pe.wait_ge(m_ptc, e + 2)
                down(MAIN, e, 16 * (e + 1))
                if first:
                    output_biases()
                more = pe.value_load(ovi[0:1, 0, bass.ds(e, 1)], min_val=0, max_val=BLOCKS - 1)
                for b in range(1, BLOCKS):
                    with pe.If(more > b - 1):
                        n = pe.value_load(ovi[0:1, 1, bass.ds(e, 1)], min_val=0, max_val=E * BLOCKS) + (b - 1)
                        gather(OVER, n)
                        gate_up(OVER, n, j, xg_o, None)
                        turn_gu(OVER, n)
                        pe.wait_ge(m_ye, e + 1)
                        turn_pt(OVER, n)
                        wait(pe, OVER, "ptc", n)
                        down(OVER, n, None)
                        wait(pe, OVER, "ye", n)
                        if first:
                            pe.wait_ge(s_bv, 4)
                        else:
                            pe.wait_ge(m_add, 2 * e)
                        scatter(OVER, n, 0, pT_o, y_o)
                        wait(pe, OVER, "add", n, 1)
                        scatter(OVER, n, 1, pT_o, y_o)
                        wait(pe, OVER, "add", n, 2)

            gather(MAIN, 0)
            turn_pt(MAIN, 0)
            for t in range(NT):
                last = nc.tensor.transpose(pb[2][0:E, t * P:(t + 1) * P], gat[:, t, :], ident[:, :])
            last.then_inc(s_gtt, 1)
            pe.wait_ge(s_nov, 1)
            mm(pb[6][:, 0:E], nov[:, 2, :], ident[0:E, 0:E])
            mm(pb[6][:, E:2 * E], nov[:, 2, :], tris[0:E, 0:E])
            mm(pb[6][:, 2 * E:3 * E], nov[:, 2, :], tri[0:E, 0:E]).then_inc(s_ov, 1)
            pe.wait_ge(s_gtv, 1)
            pe.wait_ge(m_ptc, 1)
            for e in (0, 1):
                expert(e, 0, e, e == 0, e == 1, False)
            with pe.Fori(1, E // 2 - 1) as i:
                for j in (0, 1):
                    expert(2 * i + j, i, j, False, False, False)
            for e in (E - 2, E - 1):
                expert(e, e // 2, e % 2, False, False, e == E - 1)
            pe.wait_ge(m_ye, E)
            for t in range(NT):
                pe.wait_ge(m_add, 2 * (E - 1) + t)
                scatter(MAIN, E - 1, t, pT[:, 1, :], y_s)

        @block.vector
        def _(v):
            steps = [0]

            def step(ins):
                steps[0] += 1
                ins.then_inc(dve, 1)

            def settle():
                v.wait_ge(dve, steps[0])

            V = nc.vector
            step(V.memset(uT[:, :, 0:PAD], 0.0))
            step(V.memset(ab[:, :, :], 0.0))
            step(V.memset(tok_s[:, :, :, :], 0.0))
            v.wait_ge(s_ptr, 1)
            V.tensor_copy(cols[:, :], pb[0][:, 0:N_COLS]).then_inc(s_cols, 1)
            v.wait_ge(s_ptr, 2)
            V.tensor_copy(dwc[:, :], pb[1][:, 0:WIDE * CT]).then_inc(s_cols, 1)
            v.wait_ge(s_rt, 2)
            step(V.reciprocal(st[:, 4:6], st[:, 4:6]))
            step(V.reciprocal(st[0:META, 6:7], st[0:META, 6:7]))
            settle()
            for t in range(NT):
                V.tensor_scalar(xn[:, t, :], acc[:, t, :], st[:, 4 + t:5 + t], None, ALU.mult).then_inc(s_xn, 1)
            V.tensor_scalar(xmn[0:META, :], xm[0:META, :], st[0:META, 6:7], None, ALU.mult).then_inc(s_xn, 1)
            v.wait_ge(s_cols, 2)
            for k in range(1, KT, 2):
                v.wait_ge(s_ht, k + 1)
                V.tensor_scalar(hnT[:, k, :], pb[k % 8][:, 0:SEQ], cols[:, C_NMIX + k:C_NMIX + k + 1], None, ALU.mult).then_inc(s_hv, 1)

            def short_conv(i):
                v.wait_ge(s_proj, i + 1)
                src = pb[i % PROJ_BANKS]
                dst = qkv[:, i, :]
                tap = lambda j: cols[:, C_TAP + j * 3 * H + i:C_TAP + j * 3 * H + i + 1]
                step(V.tensor_scalar(dst, src[:, 0:SEQ], tap(TAPS - 1), None, ALU.mult))
                for s in range(1, TAPS):
                    settle()
                    ins = V.scalar_tensor_tensor(out=dst[:, s:SEQ], in0=src[:, 0:SEQ - s], scalar=tap(TAPS - 1 - s), in1=dst[:, s:SEQ],
                                                 op0=ALU.mult, op1=ALU.add)
                    if s < TAPS - 1:
                        step(ins)
                    else:
                        ins.then_inc(s_conv, 1)

            def silu(r):
                v.wait_ge(s_sgq, r + 1)
                v.wait_ge(s_conv, 4 * r + 4)
                V.tensor_tensor(qkv[:, 4 * r:4 * r + 4, :], qkv[:, 4 * r:4 * r + 4, :], tmpA, ALU.mult).then_inc(s_silu, 1)

            def l2_norm(i):
                v.wait_ge(s_l2r, i + 1)
                root, r = l2_root(i), qkv[:, i, :]
                step(V.reciprocal(root, root))
                settle()
                if i < H:
                    V.scalar_tensor_tensor(out=r, in0=r, scalar=float(P) ** -0.5, in1=root, op0=ALU.mult, op1=ALU.mult).then_inc(s_qkn, 1)
                else:
                    V.tensor_tensor(r, r, root, ALU.mult).then_inc(s_qkn, 1)

            z, az, ez, lz, eb, bt, gc, kd, eg, ekd, g_, bg = (tok_s[:, i, :, :] for i in range(12))

            def decay_and_beta():
                v.wait_ge(s_aba, 4)
                v.wait_ge(s_abv, 2)
                step(V.tensor_tensor(g_, z, lz, ALU.add))
                step(V.tensor_scalar(eb, eb, 1.0, None, ALU.add))
                settle()
                step(V.reciprocal(bt, eb))
                for u in range(3):
                    step(V.scalar_tensor_tensor(out=g_[:, u, :], in0=g_[:, u, :], scalar=-1.0, in1=st[:, 8:8 + H], op0=ALU.mult, op1=ALU.mult))
                settle()
                for u, (n, c0) in enumerate(UNITS):
                    V.tensor_copy(gbc[0:n, u, :, :], g_[0:n, u, :].unsqueeze(2).to_broadcast([n, H, P])).then_inc(s_gbc, 1)
                for u, (n, c0) in enumerate(UNITS):
                    V.tensor_copy(bbc[0:n, u, :, :], bt[0:n, u, :].unsqueeze(2).to_broadcast([n, H, P])).then_inc(s_bbc, 1)

            for i in range(4):
                short_conv(i)
            v.wait_ge(s_bgutr, 1)
            for g in range(2):
                V.tensor_copy(tab[:, :, g:2 * FT:2],
                              pb[7][:, g * FT * E:(g + 1) * FT * E].rearrange("p (f e) -> p e f", f=FT)).then_inc(s_tab, 1)
            silu(0)
            for i in range(4, 8):
                short_conv(i)
            silu(1)
            for i in range(8, 12):
                short_conv(i)
                if i in (9, 10):
                    l2_norm(i - 9)
            silu(2)
            v.wait_ge(s_abm, 3)
            v.wait_ge(s_small, 48)
            settle()
            for u, (n, c0) in enumerate(UNITS):
                step(V.tensor_copy(ab[0:n, u, :], pb[7][0:n, 2 * H * u:2 * H * (u + 1)]))
            settle()
            for u in range(3):
                last = V.tensor_tensor(z[:, u, :], ab[:, u, 0:H], dtb[:, :], ALU.add)
                step(last)
            settle()
            V.scalar_tensor_tensor(out=az, in0=z, scalar=-1.0, in1=z, op0=ALU.mult, op1=ALU.max).then_inc(s_abv, 1)
            V.tensor_scalar(z, z, 0.0, None, ALU.max).then_inc(s_abv, 1)
            for i in range(2, 2 * H):
                l2_norm(i)
            decay_and_beta()
            for i in range(CT):
                v.wait_ge(s_proj, GA0 + i + 1)
                v.wait_ge(s_gb, i + 1)
                V.scalar_tensor_tensor(out=uT[:, i, PAD:PAD + SEQ], in0=pb[(GA0 + i) % PROJ_BANKS][:, 0:SEQ],
                                       scalar=cols[:, C_BGLU + i:C_BGLU + i + 1], in1=growE[:, i, :],
                                       op0=ALU.add, op1=ALU.mult).then_inc(s_ga, 1)
            for u, (n, c0) in enumerate(UNITS):
                v.wait_ge(s_gr, u + 1)
                if u == 0:
                    v.wait_ge(s_brow, 1)
                gr = heads(3 + u, n)
                for h in range(H):
                    step(V.tensor_tensor_reduce(out=gam[0:n, u, h, 0:n], in0=gr[0:n, h, :], in1=ident[0:n, 0:n], scale=1.0, scalar=0.0,
                                                op0=ALU.mult, op1=ALU.add, accum_out=gc[0:n, u, h:h + 1]))
                settle()
                for h in range(H):
                    V.tensor_scalar(gam[0:n, u, h, 0:n], gr[0:n, h, :], gc[0:n, u, h:h + 1], 0.0, ALU.subtract, ALU.min).then_inc(s_gamx, 1)
                V.tensor_tensor(kd[0:n, u, :], gr[0:n, :, n - 1], gc[0:n, u, :], ALU.subtract).then_inc(s_sm, 1)
            for u, (n, c0) in enumerate(UNITS):
                v.wait_ge(s_brow, u + 1)
                if u == 0:
                    v.wait_ge(s_qkn, 2 * H)
                V.tensor_tensor(kbT[:, :, c0:c0 + n], beta_rows(u), qkv[:, K0:K0 + H, c0:c0 + n], ALU.mult).then_inc(s_kb, 1)
            v.wait_ge(s_sme, 1)
            V.tensor_tensor(bg, bt, eg, ALU.mult).then_inc(s_smb, 1)
            v.wait_ge(s_smb, 1)
            for u, (n, c0) in enumerate(UNITS):
                v.wait_ge(s_game, u + 1)
                g3 = gam[0:n, u, :, 0:n]
                V.tensor_tensor(g3, g3, tri[0:n, 0:n].unsqueeze(1).to_broadcast([n, H, n]), ALU.mult).then_inc(s_gamm, 1)
            for u, (n, c0) in enumerate(UNITS):
                i3 = ident[0:n, 0:n].unsqueeze(1).to_broadcast([n, H, n])
                step(V.tensor_copy(inv[0:n, u, :, 0:n], i3))
                V.tensor_copy(invT[0:n, u, :, 0:n], i3).then_inc(s_lyv, 1)
            for u, (n, c0) in enumerate(UNITS):
                v.wait_ge(s_kt, 2 * u + 1)
                kb_ = 3 if u % 2 == 0 else 5
                for h in range(H):
                    V.tensor_scalar(kB[0:n, u, h, :], heads(kb_, P, n)[:, h, :], bg[0:n, u, h:h + 1], None, ALU.mult).then_inc(s_ktv, 1)
            v.wait_ge(s_gre, 2)
            for u in (1, 2):
                n, c0 = UNITS[u]
                V.tensor_tensor(qdec[:, u - 1, :, :], qkv[:, 0:H, c0:c0 + n], growE[:, :, c0:c0 + n], ALU.mult).then_inc(s_qd, 1)

            def go(i):
                v.wait_ge(s_gosig, i + 1)
                V.tensor_tensor(sgo[:, i, :], pb[(GO0 + i) % PROJ_BANKS][:, 0:TOK], scr2[:, i, :], ALU.mult).then_inc(s_go, 1)

            go(0)
            v.wait_ge(s_gamm, 3)
            for u, (n, c0) in enumerate(UNITS):
                v.wait_ge(s_at, u + 1)
                V.tensor_tensor(aT[0:n, u, :, 0:n], heads(3 + u, n, n), gam[0:n, u, :, 0:n], ALU.mult).then_inc(s_atv, 1)
            for u in (1, 2):
                v.wait_ge(s_at, 3 + u)
                V.tensor_tensor(qkT[:, u - 1, :, :], heads(5 + u), gam[:, u, :, :], ALU.mult).then_inc(s_atv, 1)
            go(1)
            go(2)
            settle()
            v.wait_ge(s_lyv, 3)
            v.wait_ge(s_pool, 2 + 2 * N_LVL)

            tapat = [0]

            def wide_taps(count):
                for _ in range(count):
                    j = tapat[0]
                    if j == WIDE:
                        return
                    tapat[0] += 1
                    if j:
                        settle()
                    else:
                        v.wait_ge(s_ga, CT)
                    for c in range(CT):
                        w = dwc[:, j * CT + c:j * CT + c + 1]
                        src = uT[:, c, j:j + TOK]
                        if j == 0:
                            ins = V.tensor_scalar(ucT[:, c, :], src, w, cols[:, C_DWB + c:C_DWB + c + 1], ALU.mult, ALU.add)
                        else:
                            ins = V.scalar_tensor_tensor(out=ucT[:, c, :], in0=src, scalar=w, in1=ucT[:, c, :], op0=ALU.mult, op1=ALU.add)
                        if j == WIDE - 1:
                            ins.then_inc(s_uc, 1)
                        else:
                            step(ins)

            for u, (n, c0) in enumerate(UNITS):
                step(V.memset(half(xlv[0:n, u, :, 0:n], 0, 1), 0.0))
            nx = ny = 0
            for l in range(N_LVL):
                settle()
                for u in lvl_units[l]:
                    n, _ = UNITS[u]
                    nx += 1
                    v.wait_ge(s_lx, nx)
                    V.tensor_tensor(half(xlv[0:n, u, :, 0:n], l, 0), packed(small_at(u, "x"), l, n),
                                    half(lvl[0:n, l, 0:n], l, 0).unsqueeze(1).to_broadcast([n, H, n >> (l + 1), 1 << l]), ALU.mult).then_inc(s_lxv, 1)
                wide_taps(2)
                for u in lvl_units[l]:
                    n, _ = UNITS[u]
                    ny += 1
                    v.wait_ge(s_ly, ny)
                    if 4 << l <= n:
                        a = half(inv[0:n, u, :, 0:n], l, 0)
                        y = packed(small_at(u, "y"), l, n) if l > 0 else half(xlv[0:n, u, :, 0:n], l, 0)
                        step(V.tensor_tensor(a, a, y, ALU.subtract))
                        settle()
                    a = half(invT[0:n, u, :, 0:n], l, 1)
                    V.tensor_tensor(a, a, packed(small_at(u, "yt"), l, n), ALU.subtract).then_inc(s_lyv, 1)
                    if 4 << l <= n:
                        step(V.memset(half(xlv[0:n, u, :, 0:n], l + 1, 1), 0.0))
                if l == 0:
                    go(3)
                wide_taps(3)
            wide_taps(WIDE)
            v.wait_ge(s_lm, 1)
            for c in range(CT):
                V.scalar_tensor_tensor(out=ucT[:, c, :], in0=pb[5][:, 0:TOK], scalar=-1.0 / (CT * P), in1=ucT[:, c, :],
                                       op0=ALU.mult, op1=ALU.add).then_inc(s_lc, 1)
            v.wait_ge(s_lr, 1)
            step(V.reciprocal(t1[:, 0:TOK], t1[:, 0:TOK]))
            settle()
            v.wait_ge(s_lc, CT)
            for c in range(CT):
                V.tensor_tensor(ucT[:, c, :], ucT[:, c, :], t1[:, 0:TOK], ALU.mult).then_inc(s_ln, 1)
            v.wait_ge(s_ln, CT)
            for c in range(CT):
                V.tensor_scalar(ucT[:, c, :], ucT[:, c, :], cols[:, C_LNG + c:C_LNG + c + 1], cols[:, C_LNB + c:C_LNB + c + 1],
                                ALU.mult, ALU.add).then_inc(s_lnz, 1)
            v.wait_ge(s_su, 1)
            v.wait_ge(s_s0a, 1)
            v.wait_ge(s_o, 1)
            c1 = META + P - 1
            for h in range(H):
                V.scalar_tensor_tensor(out=state[:, h, :], in0=state[:, h, :], scalar=growE[:, h, c1:c1 + 1], in1=heads(4)[:, h, :],
                                       op0=ALU.mult, op1=ALU.add).then_inc(s_sv, 1)
            v.wait_ge(s_lnsig, 1)
            V.tensor_tensor(ucT[:, :, :], ucT[:, :, :], scr3, ALU.mult).then_inc(s_u2, 1)

            def conv_gated(m):
                v.wait_ge(s_cb, m + 1)
                g = gates[:, KT + m, :]
                V.scalar_tensor_tensor(out=g, in0=pb[m % PROJ_BANKS][:, 0:TOK], scalar=cols[:, C_BCONV + m:C_BCONV + m + 1],
                                       in1=g, op0=ALU.add, op1=ALU.mult).then_inc(s_cm, 1)

            for u in (1, 2):
                c = slice((u - 1) * P, u * P)
                v.wait_ge(s_onr, u)
                step(V.reciprocal(scr2[:, :, c], scr2[:, :, c]))
                step(V.scalar_tensor_tensor(out=oT[:, :, c], in0=oT[:, :, c], scalar=cols[:, C_DN:C_DN + 1], in1=sgo[:, :, c],
                                            op0=ALU.mult, op1=ALU.mult))
                settle()
                V.tensor_tensor(oT[:, :, c], oT[:, :, c], scr2[:, :, c], ALU.mult).then_inc(s_og, 1)
                if u == 1:
                    conv_gated(0)
                    conv_gated(1)
                    conv_gated(2)
            for m in range(3, KT):
                conv_gated(m)
            v.wait_ge(s_cm, KT)
            for m in range(KT):
                v.wait_ge(s_ab2, m + 1)
                a = t1[:, (m % 2) * TOK:(m % 2 + 1) * TOK]
                step(V.tensor_tensor(a, pb[6 + m % 2][:, 0:TOK], gates[:, m, :], ALU.mult))
                settle()
                V.tensor_tensor(yT[:, m, :], a, gates[:, KT + m, :], ALU.add).then_inc(s_yv, 1)
            def add_out(t, c):
                v.wait_ge(s_wo, NT * t + c + 1)
                a = acc[:, t, c * 512:(c + 1) * 512]
                V.tensor_tensor(a, a, pb[2 + 2 * c + t][:, :], ALU.add).then_inc(s_wov, 1)

            def normed(t):
                v.wait_ge(s_r1, 2 * (t + 1))
                V.tensor_tensor(st[:, 12 + t:13 + t], st[:, 24 + 2 * t:25 + 2 * t], st[:, 25 + 2 * t:26 + 2 * t], ALU.add).then_inc(s_r2, 1)
                v.wait_ge(s_r3, t + 1)
                step(V.reciprocal(st[:, 14 + t:15 + t], st[:, 14 + t:15 + t]))
                settle()
                v.wait_ge(s_wov, 2 * (t + 1))
                V.tensor_scalar(hN[:, t, :], acc[:, t, :], st[:, 14 + t:15 + t], None, ALU.mult).then_inc(s_r4, 1)

            def scaled(t):
                v.wait_ge(s_r5, t + 1)
                V.tensor_tensor(hn2T[:, 0:4, t * P:(t + 1) * P], heads(6 * t), cols[:, C_NFFN:C_NFFN + 4].unsqueeze(2).to_broadcast([P, 4, P]),
                                ALU.mult).then_inc(s_hv, 1)

            def choose(t):
                v.wait_ge(s_lg, t + 1)
                step(V.tensor_tensor(lg[:, t, :], pb[2 + 2 * t][:, 0:E], brt[:, :], ALU.add))
                settle()
                step(V.max(top[:, t, :], lg[:, t, :]))
                settle()
                V.tensor_scalar(st[:, 16 + t:17 + t], top[:, t, 0:1], -1.0, None, ALU.mult).then_inc(s_msk, 1)
                step(V.max_index(topi[:, t, :], top[:, t, :], lg[:, t, :]))
                settle()
                step(V.tensor_copy(topf[:, t, :], topi[:, t, :]))
                settle()
                for k in range(TOPK):
                    idx = topf[:, t, k:k + 1]
                    if k == 0:
                        step(V.tensor_scalar(msk[:, t, :], iota[:, 0:E], idx, None, ALU.is_equal))
                    else:
                        settle()
                        ins = V.scalar_tensor_tensor(out=msk[:, t, :], in0=iota[:, 0:E], scalar=idx, in1=msk[:, t, :],
                                                     op0=ALU.is_equal, op1=ALU.add)
                        if k < TOPK - 1:
                            step(ins)
                        else:
                            ins.then_inc(s_msk, 1)

            add_out(0, 0)
            add_out(0, 1)
            normed(0)
            add_out(1, 0)
            scaled(0)
            add_out(1, 1)
            normed(1)
            v.wait_ge(s_const, 7)
            choose(0)
            scaled(1)
            choose(1)
            v.wait_ge(s_msk, 4)
            v.wait_ge(s_ex, 2)
            for t in range(NT):
                step(V.tensor_tensor_reduce(out=gat[:, t, :], in0=gat[:, t, :], in1=msk[:, t, :], scale=1.0, scalar=0.0,
                                            op0=ALU.mult, op1=ALU.add, accum_out=st[:, 18 + t:19 + t]))
            settle()
            step(V.reciprocal(st[:, 18:20], st[:, 18:20]))
            settle()
            for t in range(NT):
                V.tensor_scalar(gat[:, t, :], gat[:, t, :], st[:, 18 + t:19 + t], None, ALU.mult).then_inc(s_gt, 1)
            v.wait_ge(s_gt, 2)
            for t in range(NT):
                step(V.tensor_copy(tab[:, :, 2 * FT + NT + t], gat[:, t, :]))
            v.wait_ge(s_pos, 2)
            for t in range(NT):
                step(V.scalar_tensor_tensor(out=lg2[:, t, :], in0=pb[0][:, t * E:(t + 1) * E], scalar=1.0, in1=msk[:, t, :], op0=ALU.add, op1=ALU.mult))
            settle()
            for t in range(NT):
                step(V.tensor_scalar(tab[:, :, 2 * FT + t], lg2[:, t, :], -1.0, None, ALU.add))
            settle()
            v.wait_ge(s_tab, 2)

            gain = cols[:, C_NFFN:C_NFFN + KT].unsqueeze(2).to_broadcast([P, KT, SLOTS])

            def stage(e, n, j):
                V.tensor_copy(tabE[:, j, :], tab[:, bass.ds(e, 1), :].rearrange("p a b -> p (a b)")).then_inc(m_te, 1)
                v.wait_ge(m_te, n + 1)

            def onehots(S, b, j):
                row = iota[:, b * SLOTS:(b + 1) * SLOTS]
                for t in range(NT):
                    slot = tabE[:, j, 2 * FT + t:2 * FT + t + 1]
                    gate = tabE[:, j, 2 * FT + NT + t:2 * FT + NT + t + 1]
                    V.tensor_scalar(oh[:, t, :], row, slot, None, ALU.is_equal).then_inc(S["oh"][0], 1)
                    V.tensor_scalar(og[:, t, :].rearrange("p (a s) -> p a s", a=2), row.unsqueeze(1).to_broadcast([P, 2, SLOTS]),
                                    slot, gate, ALU.is_equal, ALU.mult).then_inc(S["oh"][0], 1)

            def xg_copy(S, n, dst):
                wait(v, S, "ga", n)
                V.tensor_tensor(dst, pb[4].rearrange("p (k s) -> p k s", k=KT), gain, ALU.mult).then_inc(S["xg"][0], 1)

            def gu_copy(S, n):
                wait(v, S, "gu", n)
                V.tensor_copy(gu_s[:, 512:1024], pb[1]).then_inc(S["ev"][0], 1)

            def bias_clip(S, n, j):
                wait(v, S, "t", n)
                bias = tabE[:, j, 0:2 * FT].rearrange("p (f g) -> p f g", g=2)
                for b in range(2):
                    f = slice(b * FT // 2, (b + 1) * FT // 2)
                    V.tensor_tensor(tS[:, f, :, :], pb[2 + b].rearrange("p (f g s) -> p f g s", f=FT // 2, g=2),
                                    bias[:, f, :].unsqueeze(3).to_broadcast([P, FT // 2, 2, SLOTS]), ALU.add).then_inc(S["tb"][0], 1)
                wait(v, S, "tb", n, 2)
                V.tensor_scalar(tS[:, :, 0, :], tS[:, :, 0, :], 7.0, None, ALU.min).then_inc(S["g"][0], 1)
                V.tensor_scalar(tS[:, :, 1, :], tS[:, :, 1, :], 7.0, -7.0, ALU.min, ALU.max).then_inc(S["up"][0], 1)

            def swiglu(S, n):
                wait(v, S, "up", n)
                V.scalar_tensor_tensor(out=hid[:, :, :], in0=tS[:, :, 1, :], scalar=1.0, in1=tS[:, :, 0, :],
                                       op0=ALU.add, op1=ALU.mult).then_inc(S["a"][0], 1)
                wait(v, S, "a", n)
                wait(v, S, "sig", n)
                V.tensor_tensor(hid[:, :, :], hid[:, :, :], sg[:, :, :], ALU.mult).then_inc(S["hid"][0], 1)

            def add(S, n, t):
                wait(v, S, "sc", n, t + 1)
                a = acc[:, t, :].rearrange("p (c d) -> p c d", c=2)
                V.tensor_tensor(a, a, psum[:, 6:8, :], ALU.add).then_inc(S["add"][0], 1)

            def add_output_biases():
                for t in range(NT):
                    for c in range(2):
                        v.wait_ge(s_bm, 2 * t + c + 1)
                        a = acc[:, t, c * 512:(c + 1) * 512]
                        V.tensor_tensor(a, a, pb[6 + c], ALU.add).then_inc(s_bv, 1)
                v.wait_ge(s_bv, 4)

            def expert(e, j, first, last):
                if not last:
                    stage(e + 1, e + 1, 1 - j)
                    v.wait_ge(m_pt, e + 1)
                    onehots(MAIN, 0, 1 - j)
                gu_copy(MAIN, e)
                if not first:
                    add(MAIN, e - 1, 0)
                bias_clip(MAIN, e, j)
                if not last:
                    xg_copy(MAIN, e + 1, xg)
                swiglu(MAIN, e)
                if first:
                    add_output_biases()
                else:
                    add(MAIN, e - 1, 1)
                    v.wait_ge(m_add, 2 * e)
                more = v.value_load(ovi[0:1, 0, bass.ds(e, 1)], min_val=0, max_val=BLOCKS - 1)
                for b in range(1, BLOCKS):
                    with v.If(more > b - 1):
                        n = v.value_load(ovi[0:1, 1, bass.ds(e, 1)], min_val=0, max_val=E * BLOCKS) + (b - 1)
                        v.wait_ge(m_pt, e + (1 if last else 2))
                        wait(v, MAIN, "hid", e)
                        onehots(OVER, b, j)
                        xg_copy(OVER, n, xg_o)
                        gu_copy(OVER, n)
                        bias_clip(OVER, n, j)
                        swiglu(OVER, n)
                        for t in range(NT):
                            add(OVER, n, t)
                        wait(v, OVER, "add", n, 2)
                        v.sem_inc(s_over, 1)

            stage(0, 0, 0)
            onehots(MAIN, 0, 0)
            for b in range(1, BLOCKS):
                step(V.tensor_scalar(nov[:, b - 1, :], pb[3][0:E, 0:P], float(SLOTS * b), None, ALU.is_gt))
            settle()
            step(V.tensor_tensor(nov[:, 0, :], nov[:, 0, :], nov[:, 1, :], ALU.add))
            settle()
            V.tensor_tensor(nov[:, 2, :], nov[:, 0, :], nov[:, 2, :], ALU.add).then_inc(s_nov, 1)
            xg_copy(MAIN, 0, xg)
            v.wait_ge(s_ov, 1)
            V.tensor_copy(ovi[:, 0:2, :], pb[6][:, 0:2 * E].rearrange("p (a e) -> p a e", a=2)).then_inc(s_ovv, 1)
            V.tensor_scalar(ovi[:, 2, :], pb[6][:, 2 * E:3 * E], 1.0, 0.0, ALU.subtract, ALU.max).then_inc(s_ovv, 1)
            v.wait_ge(s_ovv, 2)
            for e in (0, 1):
                expert(e, e, e == 0, False)
            with v.Fori(1, E // 2 - 1) as i:
                for j in (0, 1):
                    expert(2 * i + j, j, False, False)
            for e in (E - 2, E - 1):
                expert(e, e % 2, False, e == E - 1)
            for t in range(NT):
                add(MAIN, E - 1, t)
            v.wait_ge(s_gf, 16)
            v.wait_ge(m_add, 2 * E)
            for t in range(NT):
                v.wait_ge(s_f3, t + 1)
                step(V.reciprocal(st[:, 22 + t:23 + t], st[:, 22 + t:23 + t]))
                settle()
                V.scalar_tensor_tensor(out=acc[:, t, :], in0=acc[:, t, :], scalar=st[:, 22 + t:23 + t], in1=gu_w[0][0][:, 0:D],
                                       op0=ALU.mult, op1=ALU.mult).then_inc(s_f4, 1)


_INS = ['x', 'meta_tokens', 'norm_mix_g', 'w_in', 'conv_qkv_w', 'a_log', 'dt_bias', 'dn_norm_g', 'w_dn_out',
        'b_glu', 'conv_dw_w', 'conv_dw_b', 'conv_ln_g', 'conv_ln_b', 'w_conv_out', 'b_conv_out', 'w_merge',
        'b_merge', 'w_out', 'norm_ffn_g', 'w_router', 'b_router', 'w_gate_up', 'b_gate_up', 'w_down', 'b_down',
        'final_norm_g']
_OUT = (1, 256, 1024)


def kernel(**inputs):
    import numpy as _np
    import concourse.bacc as _bacc
    from concourse import mybir as _mybir
    from concourse.bass_utils import run_bass_kernel_spmd as _run

    nc = _bacc.Bacc("TRN2", target_bir_lowering=False, num_devices=1)
    arrays, args = {}, []
    for name in _INS:
        a = _np.ascontiguousarray(inputs[name])
        arrays[f"in_{name}"] = a
        args.append(nc.dram_tensor(f"in_{name}", a.shape, _mybir.dt.from_np(a.dtype), kind="ExternalInput").ap())
    args.append(nc.dram_tensor("out_0", _OUT, _mybir.dt.float32, kind="ExternalOutput").ap())
    build(nc, *args)
    r = _run(nc, [arrays], core_ids=[0])
    return r.results[0]["out_0"]
```
